# Optimizing a Trainium2 kernel written in Bass

```python
import jax, jax.numpy as jnp
from jax import lax
import numpy as np

D_MODEL = 2048
BATCH = 1
SEQ = 512
DEPTH = 1
DEC_BATCH = 8
DEC_SEQ = 8
PAST_LEN = 512
PAGE_SIZE = 128

H_RET = 8
DK_RET = 128
DV_RET = 256
RET_CHUNK = 128
H_SB = 8
D_SB = 128
SB_BLOCK = 128
SB_BIAS_INIT = -8.0
ROPE_BASE = 10000.0
EPS_RMS = 1e-6
EPS_GN = 1e-5
W_RET_QK = H_RET * DK_RET
W_RET_V = H_RET * DV_RET
W_SB = H_SB * D_SB
SPLITS = (W_RET_QK, W_RET_QK, W_RET_V, W_RET_V, W_SB, W_SB, W_SB, W_SB, D_MODEL, D_MODEL)
IN_COLS = 2 * W_RET_QK + 2 * W_RET_V + 4 * W_SB + 2 * D_MODEL

kernel_name = 'retention_stickbreaking_gated_hybrid_step'

def rmsnorm(x, g):
    xf = x.astype(jnp.float32)
    r = lax.rsqrt(jnp.mean(xf * xf, axis=-1, keepdims=True) + EPS_RMS)
    return (xf * r * g.astype(jnp.float32)).astype(x.dtype)

def rope(x, pos):
    half = x.shape[-1] // 2
    inv = ROPE_BASE ** (-jnp.arange(half, dtype=jnp.float32) / half)
    ang = pos.astype(jnp.float32)[:, None] * inv[None, :]
    cos = jnp.cos(ang)[None, :, None, :]
    sin = jnp.sin(ang)[None, :, None, :]
    x1 = x[..., :half].astype(jnp.float32)
    x2 = x[..., half:].astype(jnp.float32)
    return jnp.concatenate([x1 * cos - x2 * sin, x2 * cos + x1 * sin], axis=-1)

def ret_log_gamma():
    return jnp.log1p(-jnp.exp2(-5.0 - jnp.arange(H_RET, dtype=jnp.float32)))

def retention_chunk(S, q, k, v):
    lg = ret_log_gamma()
    C = q.shape[1]
    S = S.astype(jnp.float32)
    q = q.astype(jnp.float32)
    k = k.astype(jnp.float32)
    v = v.astype(jnp.float32)
    idx = jnp.arange(C, dtype=jnp.float32)
    diff = idx[:, None] - idx[None, :]
    decay = jnp.where(diff >= 0, jnp.exp(lg[:, None, None] * jnp.maximum(diff, 0.0)[None]), 0.0)
    inner = jnp.einsum('bihd,bjhd->bhij', q, k) * decay[None]
    o_inner = jnp.einsum('bhij,bjhe->bihe', inner, v)
    cross_decay = jnp.exp(lg[:, None] * (idx + 1.0)[None, :]).T
    o_cross = jnp.einsum('bihd,bhde->bihe', q, S) * cross_decay[None, :, :, None]
    k_decay = jnp.exp(lg[:, None] * (C - 1.0 - idx)[None, :]).T
    S_new = jnp.exp(lg * C)[None, :, None, None] * S + jnp.einsum('bjhd,bjhe->bhde', k * k_decay[None, :, :, None], v)
    return S_new, o_inner + o_cross

def stick_breaking(q, k, v, q_pos, k_pos, bias):
    z = jnp.einsum('bqhd,bkhd->bhqk', q.astype(jnp.float32), k.astype(jnp.float32)) * (D_SB ** -0.5)
    z = z + bias.astype(jnp.float32)[None, :, None, None]
    mask = (k_pos[None, :] < q_pos[:, None])[None, None]
    log_keep = jnp.where(mask, jax.nn.log_sigmoid(-z), 0.0)
    after = lax.cumsum(log_keep, axis=3, reverse=True) - log_keep
    a = jnp.where(mask, jnp.exp(jax.nn.log_sigmoid(z) + after), 0.0)
    return jnp.einsum('bhqk,bkhd->bqhd', a, v.astype(jnp.float32))

def project(xn, w_in):
    cuts = [int(c) for c in np.cumsum(SPLITS)[:-1]]
    return jnp.split(xn @ w_in, cuts, axis=-1)

def ret_qkv(rq, rk, rv, pos):
    B, T = rq.shape[:2]
    q = rope(rq.reshape(B, T, H_RET, DK_RET), pos)
    k = rope(rk.reshape(B, T, H_RET, DK_RET), pos) * (DK_RET ** -0.5)
    v = rv.reshape(B, T, H_RET, DV_RET)
    return q, k, v

def merge_out(x, o_ret, g_ret, o_sb, g_sb, gate_r, gate_s, ret_gn_gain, w_ret_proj, w_sb_proj, w_out):
    B, T = x.shape[:2]
    o = o_ret.astype(jnp.float32)
    mu = jnp.mean(o, axis=-1, keepdims=True)
    var = jnp.mean(jnp.square(o - mu), axis=-1, keepdims=True)
    o = ((o - mu) * lax.rsqrt(var + EPS_GN)).reshape(B, T, W_RET_V) * ret_gn_gain.astype(jnp.float32)
    ret_branch = (o * jax.nn.silu(g_ret.astype(jnp.float32))).astype(x.dtype)
    sb_branch = (o_sb.reshape(B, T, W_SB) * jax.nn.silu(g_sb.astype(jnp.float32))).astype(x.dtype)
    merged = jax.nn.sigmoid(gate_r) * (ret_branch @ w_ret_proj) + jax.nn.sigmoid(gate_s) * (sb_branch @ w_sb_proj)
    return x + merged @ w_out

def prompt_layer(x, norm_gain, w_in, sb_bias, ret_gn_gain, w_ret_proj, w_sb_proj, w_out):
    B, T = x.shape[:2]
    xn = rmsnorm(x, norm_gain)
    rq, rk, rv, rg, sq, sk, sv, sg, gr, gs = project(xn, w_in)
    pos = jnp.arange(T, dtype=jnp.int32)
    q, k, v = ret_qkv(rq, rk, rv, pos)
    nc = T // RET_CHUNK
    to_chunks = lambda a: a.reshape(B, nc, RET_CHUNK, *a.shape[2:]).swapaxes(0, 1)
    S0 = jnp.zeros((B, H_RET, DK_RET, DV_RET), jnp.float32)
    S_fin, o = lax.scan(lambda S, xs: retention_chunk(S, xs[0], xs[1], xs[2]), S0,
                        (to_chunks(q), to_chunks(k), to_chunks(v)))
    o_ret = o.swapaxes(0, 1).reshape(B, T, H_RET, DV_RET)
    sq = sq.reshape(B, T, H_SB, D_SB)
    sk = sk.reshape(B, T, H_SB, D_SB)
    sv = sv.reshape(B, T, H_SB, D_SB)
    nb = T // SB_BLOCK
    qb = sq.reshape(B, nb, SB_BLOCK, H_SB, D_SB).swapaxes(0, 1)
    posb = pos.reshape(nb, SB_BLOCK)
    o_sb = lax.map(lambda a: stick_breaking(a[0], sk, sv, a[1], pos, sb_bias), (qb, posb))
    o_sb = o_sb.swapaxes(0, 1).reshape(B, T, H_SB, D_SB)
    h = merge_out(x, o_ret, rg, o_sb, sg, gr, gs, ret_gn_gain, w_ret_proj, w_sb_proj, w_out)
    return h, S_fin, sk, sv

def sample_layer(x, S_past, pool_k, pool_v, page_table, norm_gain, w_in, sb_bias, ret_gn_gain, w_ret_proj, w_sb_proj, w_out):
    B, T = x.shape[:2]
    past_len = page_table.shape[1] * pool_k.shape[1]
    xn = rmsnorm(x, norm_gain)
    rq, rk, rv, rg, sq, sk, sv, sg, gr, gs = project(xn, w_in)
    pos = past_len + jnp.arange(T, dtype=jnp.int32)
    q, k, v = ret_qkv(rq, rk, rv, pos)
    S_new, o_ret = retention_chunk(S_past, q, k, v)
    sq = sq.reshape(B, T, H_SB, D_SB)
    sk = sk.reshape(B, T, H_SB, D_SB)
    sv = sv.reshape(B, T, H_SB, D_SB)
    past_k = pool_k[page_table].reshape(B, past_len, H_SB, D_SB)
    past_v = pool_v[page_table].reshape(B, past_len, H_SB, D_SB)
    keys = jnp.concatenate([past_k, sk.astype(past_k.dtype)], axis=1)
    vals = jnp.concatenate([past_v, sv.astype(past_v.dtype)], axis=1)
    k_pos = jnp.arange(past_len + T, dtype=jnp.int32)
    o_sb = stick_breaking(sq, keys, vals, pos, k_pos, sb_bias)
    h = merge_out(x, o_ret, rg, o_sb, sg, gr, gs, ret_gn_gain, w_ret_proj, w_sb_proj, w_out)
    return h, S_new, sk, sv

def setup_inputs(seed: int = 0) -> dict:
    key = jax.random.key(seed)
    ks = jax.random.split(key, 14)
    n_pages = PAST_LEN // PAGE_SIZE
    n_used = DEC_BATCH * n_pages
    n_pool = n_used + n_used // 4
    f32 = jnp.float32
    x_prompt = jax.random.normal(ks[0], (BATCH, SEQ, D_MODEL), f32)
    x_sample = jax.random.normal(ks[1], (DEC_BATCH, DEC_SEQ, D_MODEL), f32)
    state_ret = 0.5 * jax.random.normal(ks[2], (DEPTH, DEC_BATCH, H_RET, DK_RET, DV_RET), f32)
    cache_sb_k = jax.random.normal(ks[3], (DEPTH, n_pool, PAGE_SIZE, H_SB, D_SB), f32)
    cache_sb_v = jax.random.normal(ks[4], (DEPTH, n_pool, PAGE_SIZE, H_SB, D_SB), f32)
    page_table = jax.random.permutation(ks[5], n_pool)[:n_used].reshape(DEC_BATCH, n_pages).astype(jnp.int32)
    norm_gain = 1.0 + 0.01 * jax.random.normal(ks[6], (DEPTH, D_MODEL), f32)
    w_in = jax.random.normal(ks[7], (DEPTH, D_MODEL, IN_COLS), f32) * D_MODEL ** -0.5
    sb_bias = SB_BIAS_INIT + 0.1 * jax.random.normal(ks[13], (DEPTH, H_SB), f32)
    ret_gn_gain = 1.0 + 0.01 * jax.random.normal(ks[8], (DEPTH, W_RET_V), f32)
    w_ret_proj = jax.random.normal(ks[9], (DEPTH, W_RET_V, D_MODEL), f32) * W_RET_V ** -0.5
    w_sb_proj = jax.random.normal(ks[10], (DEPTH, W_SB, D_MODEL), f32) * W_SB ** -0.5
    w_out = jax.random.normal(ks[11], (DEPTH, D_MODEL, D_MODEL), f32) * D_MODEL ** -0.5
    final_norm_gain = 1.0 + 0.01 * jax.random.normal(ks[12], (D_MODEL,), f32)
    return {'x_prompt': x_prompt, 'x_sample': x_sample, 'state_ret': state_ret,
            'cache_sb_k': cache_sb_k, 'cache_sb_v': cache_sb_v, 'page_table': page_table,
            'norm_gain': norm_gain, 'w_in': w_in, 'sb_bias': sb_bias, 'ret_gn_gain': ret_gn_gain,
            'w_ret_proj': w_ret_proj, 'w_sb_proj': w_sb_proj, 'w_out': w_out,
            'final_norm_gain': final_norm_gain}

def reference(x_prompt, x_sample, state_ret, cache_sb_k, cache_sb_v, page_table,
              norm_gain, w_in, sb_bias, ret_gn_gain, w_ret_proj, w_sb_proj, w_out, final_norm_gain):
    hp = x_prompt
    hs = x_sample
    ret_p, k_p, v_p, ret_s, k_s, v_s = [], [], [], [], [], []
    for l in range(DEPTH):
        hp, S_p, sk_p, sv_p = prompt_layer(hp, norm_gain[l], w_in[l], sb_bias[l], ret_gn_gain[l],
                                           w_ret_proj[l], w_sb_proj[l], w_out[l])
        hs, S_s, sk_s, sv_s = sample_layer(hs, state_ret[l], cache_sb_k[l], cache_sb_v[l], page_table,
                                           norm_gain[l], w_in[l], sb_bias[l], ret_gn_gain[l],
                                           w_ret_proj[l], w_sb_proj[l], w_out[l])
        ret_p.append(S_p)
        k_p.append(sk_p)
        v_p.append(sv_p)
        ret_s.append(S_s)
        k_s.append(sk_s)
        v_s.append(sv_s)
    y_prompt = rmsnorm(hp, final_norm_gain)
    y_sample = rmsnorm(hs, final_norm_gain)
    return (y_prompt, y_sample, jnp.stack(ret_p), jnp.stack(k_p), jnp.stack(v_p),
            jnp.stack(ret_s), jnp.stack(k_s), jnp.stack(v_s))


_drawn_inputs = setup_inputs


def setup_inputs(seed=0):
    import zlib

    import numpy as np

    out = dict(_drawn_inputs(seed))
    spreads = {}
    factors = {'cache_sb_k': 8.0,
     'cache_sb_v': 8.0,
     'norm_gain': 3.785,
     'sb_bias': 8.0,
     'ret_gn_gain': 8.0,
     'w_sb_proj': 8.0,
     'final_norm_gain': 5.807}
    for name, (base, spread) in spreads.items():
        noise = np.random.default_rng([zlib.crc32(name.encode()), seed]).standard_normal(out[name].shape)
        drawn = base * np.exp(spread * noise) if base else spread * noise
        out[name] = __import__('jax').numpy.asarray(drawn.astype(out[name].dtype))
    for name, factor in factors.items():
        out[name] = (out[name] * factor).astype(out[name].dtype)
    return out
```

```python
from contextlib import ExitStack

import numpy as np

import concourse.bass as bass
from concourse import mybir

F32 = mybir.dt.float32
F32R = mybir.dt.float32r
I32 = mybir.dt.int32
ALU = mybir.AluOpType
ACT = mybir.ActivationFunctionType

P = 128
D_MODEL = 2048
SEQ = 512
NB, TS = 8, 8
NS = NB * TS
T = SEQ + NS
HALF = T // 2
H = 8
D = 128
DV = 256
PAGES = 4
KT = D_MODEL // P
QK = 4
C_RQ, C_RK, C_RV, C_RG = 0, 1024, 2048, 4096
C_SQ, C_SK, C_SV, C_SG, C_GR, C_GS = 6144, 7168, 8192, 9216, 10240, 12288
SCALE = float(D) ** -0.5
EPS_RMS, EPS_GN = 1e-6, 1e-5
BIG = 1e38
NO = -1e30
SEG = [(0, 512), (512, 384), (896, 384)]
BLK = [(0, 512), (512, 384), (896, 256), (1152, 128)]
ZS0, ZN0, ZW = 1280, 1536, 1600
T_DP, T_DS, T_KP, T_KS, T_GC, T_G8, T_QP, T_QS, T_W = 0, 128, 192, 193, 201, 202, 203, 331, 339

_W = {f"{n}{s}": k for n, k, r in (("raw_in", 16, 2), ("raw_free", 1, 2), ("hi_full", 1, 4), ("w_full", 1, 4),
                                   ("w_free", 1, 4)) for s in range(r)}


def per(loads, act0=0, act1=0, dve0=0, dve1=0, **more):
    out = {k: v * (loads // 2) for k, v in _W.items()}
    return out | {"acc_act0": act0, "acc_act1": act1, "acc_dve0": dve0, "acc_dve1": dve1,
                  "acc_read0": act0 + dve0, "acc_read1": act1 + dve1} | more


PER_SB = per(8, act0=2, act1=2, z_act0=6, z_act1=1, z_act2=1, z_act3=1, z_dve1=5, z_dve2=6, z_dve3=1,
             z_read0=6, z_read1=6, z_read2=7, z_read3=2, q_ev=1, k_ev=1, v_ev=1, qs=1, zs_ready=4, w_abs=4,
             w_ln=4, l_raw=4, l_ready=4, x_raw=4, x_ready=4, a_ready=4, t_ready=2, rh_done=2, ge=1, kv_out=64, vn=2,
             **{f"k_in{b}": 64 for b in range(8)}, **{f"v_in{b}": 64 for b in range(8)})
PER_GATE = per(4, act0=1, act1=1, ge=2, sg_ready=2, sg_out0=16, sg_out1=16)
PER_PSB = per(4, dve0=2, dve1=2, gs_in0=32, gs_in1=32, m_ready=4, m_out0=32, m_out1=32)
PER_RET = per(12, act0=2, act1=2, dve0=1, dve1=1, z_act1=1, z_act2=2, z_dve0=3, z_dve1=3, z_dve2=5, z_dve3=4,
              z_read0=3, z_read1=4, z_read2=7, z_read3=4, q_ev=1, k_ev=1, v_ev=2, tab_in=16, tab_used=1, gain_in=16,
              gain_used=1, qd=1, p_ready=2, kd=1, km=1, s_ready=1, st_in0=64, st_in1=64, st_new=4, st_out0=64,
              st_out1=64, vn=4, stat=5, rstd=5, on=5, t_ready=4, rh_done=4, ge=2, rgt_read=2, s_out=16)
PER_C = per(4, dve0=1, dve1=1, mg_in0=32, mg_in1=32, mg_used=2, t_ready=2, rh_done=2)
PER_D = per(4, act0=1, act1=1, y_ev=2, z_dve0=1, z_dve1=1, z_dve2=1, z_dve3=1, z_read0=1, z_read1=1, z_read2=1,
            z_read3=1)


class Tally:

    def __init__(self, eng, sems):
        self.eng, self.sems, self.n, self.loop = eng, sems, {}, None

    def value(self, name):
        n = self.n.get(name, 0)
        if self.loop is None:
            return n
        i, first, each, _ = self.loop
        return i * each.get(name, 0) + (n - first * each.get(name, 0))

    def take(self, name, k=1):
        self.n[name] = self.n.get(name, 0) + k
        self.eng.wait_ge(self.sems[name], self.value(name))

    def room(self, name, k=1):
        v = self.value(name)
        if not (isinstance(v, int) and v <= 0):
            self.eng.wait_ge(self.sems[name], v)
        self.n[name] = self.n.get(name, 0) + k

    def reach(self, name):
        self.eng.wait_ge(self.sems[name], self.value(name))

    def settle(self):
        self.eng.sem_inc(self.sems["settled"], 1)

    def skip(self, name, k=1):
        self.n[name] = self.n.get(name, 0) + k

    def enter(self, i, first, each):
        self.loop = (i, first, each, dict(self.n))

    def leave(self, turns):
        _, _, each, before = self.loop
        for name, n in self.n.items():
            one = n - before.get(name, 0)
            assert one == (each.get(name, 0) if one else 0), (name, one, each.get(name, 0))
            self.n[name] = before.get(name, 0) + one * turns
        self.loop = None


def build(nc, x_prompt, x_sample, state_ret, cache_k, cache_v, page_table, norm_gain, w_in, sb_bias, gn_gain,
          w_ret, w_sb, w_out, final_gain, c_mats, c_rope, c_tab,
          y_prompt, y_sample, ret_p, sbk_p, sbv_p, ret_s, sbk_s, sbv_s):
    ctx = ExitStack()
    with ctx:
        names = sorted(set(PER_SB) | set(PER_GATE) | set(PER_PSB) | set(PER_RET) | set(PER_C) | set(PER_D)
                       | {"consts", "vecs", "pt_in", "x_in0", "x_in1", "x_in2", "x_in3", "x_in4", "rs0", "xs_ready",
                          "x_t", "xh_done", "xl_done", "h_in", "lows_done", "fg_in", "rs_f", "y_done", "y_out", "settled",
                          "rope_in"})
        S = {n: ctx.enter_context(nc.semaphore(n)) for n in names}

        top = [1152]

        def sb(name, shape, dt=F32, at=None):
            size = int(np.prod(shape[1:])) * 4
            if at is None:
                at = top[0]
                top[0] = at + (size + 31) // 32 * 32
            return nc.alloc_sbuf_tensor_at(name, list(shape), dt, offset=at), at + (size + 31) // 32 * 32

        XH, _ = sb("XH", [P, KT, T], F32R)
        XL, _ = sb("XL", [P, KT, T], F32R)
        rh_at = top[0]
        RH, _ = sb("RH", [P, KT, T], F32R)
        RL, _ = sb("RL", [P, KT, T], F32R)
        RAW, _ = sb("RAW", [P, 2, 8, P])
        HI, _ = sb("HI", [P, 4, QK, P], F32R)
        LO, _ = sb("LO", [P, 4, QK, P], F32R)
        MATS, _ = sb("MATS", [P, 3, P])
        NG, _ = sb("NG", [P, KT])
        SBB, _ = sb("SBB", [P, H])
        BIAS, _ = sb("BIAS", [P, 1])
        PT, _ = sb("PT", [1, NB * PAGES], I32)
        SSQ, _ = sb("SSQ", [P, 8])
        RSTD, _ = sb("RSTD", [P, 8])
        IDENT, UPPER, ONES = MATS[:, 0, :], MATS[:, 1, :], MATS[:, 2, :]
        ws = top[0]
        XN, _ = sb("XN", [P, 5, D_MODEL], at=ws)
        JUNK, _ = sb("JUNK", [P, D_MODEL], at=rh_at)
        XT, _ = sb("XT", [P, 2, 4, P], at=rh_at + 8192)
        KTR, _ = sb("KTR", [P, 4, 4 * P], at=rh_at + 8 * T * 4)
        VC, _ = sb("VC", [P, NB, 4 * P], at=rh_at + KT * T * 4 + 8 * T * 4)
        at = ws
        KC, at = sb("KC", [P, NB, 4 * P], at=at)
        QT, at = sb("QT", [P, T], at=at)
        KTT, at = sb("KTT", [P, T], at=at)
        VT, at = sb("VT", [P, T], at=at)
        QS, at = sb("QS", [P, NS], at=at)
        KN, at = sb("KN", [P, 5, P], at=at)
        VN, at = sb("VN", [P, 5, P], at=at)
        ZZ, at = sb("ZZ", [P, ZW], at=at)
        LL, at = sb("LL", [P, ZW], at=at)
        GG, at = sb("GG", [P, T], at=at)
        GT, at = sb("GT", [P, T], at=at)
        TT, at = sb("TT", [P, T], at=at)
        SG, at = sb("SG", [P, 2, T], at=at)
        assert at <= 229344, at
        GSI, at = sb("GSI", [P, 2, T], at=ws)
        MO, at = sb("MO", [P, 2, T], at=at)
        at = ws
        RCOS, at = sb("RCOS", [P, T], at=at)
        RSIN, at = sb("RSIN", [P, T], at=at)
        SG2, _ = sb("SG2", [P, 2, T], at=ws)
        RQT, at = sb("RQT", [P, T], at=at)
        RKT, at = sb("RKT", [P, T], at=at)
        RT, at = sb("RT", [P, T], at=at)
        TAB, at = sb("TAB", [P, T_W], at=at)
        GN2, at = sb("GN2", [P, 2], at=at)
        RVT, at = sb("RVT", [P, T], at=at)
        RVN, at = sb("RVN", [P, 5, DV], at=at)
        KD, at = sb("KD", [P, 4, P], at=at)
        KM, at = sb("KM", [NS, NB, P], at=at)
        RG, at = sb("RG", [P, 2, T], at=at)
        RGT, at = sb("RGT", [P, T], at=at)
        SP_, at = sb("SP_", [P, 4, DV], at=at)
        ST, at = sb("ST", [P, 2, 2, DV], at=at)
        QM, at = sb("QM", [P, NB, NS], at=at)
        QD, at = sb("QD", [P, 3, P], at=at)
        PR, at = sb("PR", [P, 4, P], at=at)
        PS, at = sb("PS", [NS, NS], at=at)
        ON, at = sb("ON", [P, 5, DV], at=at)
        STAT, at = sb("STAT", [P, 5, 6], at=at)
        MV, at = sb("MV", [P, 5, 2], at=at)
        RS5, at = sb("RS5", [P, 5], at=at)
        assert at <= 229344, at
        MGI, at = sb("MGI", [P, 2, 2, T], at=ws)
        MT, at = sb("MT", [P, T], at=at)
        HH, _ = sb("HH", [P, 5, D_MODEL], at=rh_at)
        YT, at = sb("YT", [P, 2, T], at=at)
        FG, at = sb("FG", [P, D_MODEL], at=at)
        JF, at = sb("JF", [P, D_MODEL], at=at)
        assert at <= 229344, at

        ACC = [ctx.enter_context(nc.psum_tensor(f"ACC{s}", [P, 2, 512], F32)) for s in range(2)]
        Z = [ctx.enter_context(nc.psum_tensor(f"Z{s}", [P, 512], F32)) for s in range(4)]

        def acc(s):
            return ACC[s][:, :, 0:HALF]

        def two(ap):
            return ap.rearrange("p (a b) -> p a b", a=2)

        d_gs = nc.dram_tensor("scratch_gate_s", (KT, P, T), F32).ap()
        d_gr = nc.dram_tensor("scratch_gate_r", (KT, P, T), F32).ap()
        d_m = nc.dram_tensor("scratch_merge_s", (KT, P, T), F32).ap()
        block = ctx.enter_context(nc.Block())

        @block.sync
        def _(sp):
            t = Tally(sp, S)
            rot = [0]

            def weights(w, col, half):
                s = rot[0] % 2
                rot[0] += 1
                t.room(f"raw_free{s}")
                src = w[half * 1024:(half + 1) * 1024, bass.ds(col, P)].rearrange("(k p) n -> p k n", p=P)
                sp.dma_start(RAW[:, s], src).then_inc(S[f"raw_in{s}"], 16)

            sp.dma_start(MATS[:], c_mats).then_inc(S["consts"], 16)
            for n in range(4):
                sp.dma_start(XN[:, n, :], x_prompt[0, n * P:(n + 1) * P, :]).then_inc(S[f"x_in{n}"], 16)
            sp.dma_start(XN[0:NS, 4, :], x_sample.rearrange("b t n -> (b t) n")).then_inc(S["x_in4"], 16)
            sp.dma_start(NG[:], norm_gain.rearrange("o (k p) -> p (o k)", p=P),
                         allow_slow_non_contiguous=True).then_inc(S["vecs"], 16)
            sp.dma_start(SBB[:], sb_bias[0:1, :].broadcast_to([P, H])).then_inc(S["vecs"], 16)
            sp.dma_start(PT[:], page_table.rearrange("b (o n) -> o (b n)", o=1)).then_inc(S["pt_in"], 16)
            sp.wait_ge(S["pt_in"], 16)
            page = [sp.value_load(PT[0:1, k:k + 1], min_val=0, max_val=cache_k.shape[1] - 1)
                    for k in range(NB * PAGES)]

            def keys(h):
                for b in range(NB):
                    for g in range(PAGES):
                        sp.dma_start(KC[:, b, g * P:(g + 1) * P], cache_k[0, page[b * PAGES + g], :, h, :])\
                            .then_inc(S[f"k_in{b}"], 16)

            def values(h):
                for b in range(NB):
                    for g in range(PAGES):
                        sp.dma_start(VC[:, b, g * P:(g + 1) * P], cache_v[0, page[b * PAGES + g], :, h, :])\
                            .then_inc(S[f"v_in{b}"], 16)

            def kv_out(h):
                for g in range(3):
                    t.reach(f"z_read{g}")
                for src, dp, ds_ in ((KN, sbk_p, sbk_s), (VN, sbv_p, sbv_s)):
                    sp.dma_start(dp[0, 0, :, h, :].rearrange("(n p) d -> p n d", p=P), src[:, 0:4, :])\
                        .then_inc(S["kv_out"], 16)
                    sp.dma_start(ds_[0].rearrange("b t h d -> (b t) h d")[:, h, :], src[0:NS, 4, :])\
                        .then_inc(S["kv_out"], 16)

            def sb_body(h, a):
                for p in range(8):
                    weights(w_in[0], (C_SQ, C_SK, C_SV, C_SG)[p // 2] + h * P, p % 2)
                    if p == 2 and a is not None:
                        kv_out(a)
                        values(a)
                    if p == 6:
                        if a is not None:
                            t.take("z_read0", 5)
                            t.take("z_read1", 5)
                        keys(h)
                t.skip("z_read0")
                t.skip("z_read1")
                t.skip("z_read2", 1 if a is None else 7)

            for g in range(3):
                t.skip(f"z_read{g}", 5)
            sb_body(0, None)
            with sp.Fori(1, H) as i:
                t.enter(i, 1, PER_SB)
                sb_body(i, i - 1)
                t.leave(H - 1)

            gate_n = [0]

            def gate_out(c, dst):
                s = gate_n[0] % 2
                gate_n[0] += 1
                t.take("sg_ready")
                src = (SG if dst is d_gs else SG2)[:, s, :]
                sp.dma_start(dst[c], src).then_inc(S[f"sg_out{s}"], 16)

            for c in range(4):
                for p in range(2):
                    weights(w_in[0], C_GS + c * P, p)
                    if c == 1 and p == 0:
                        kv_out(H - 1)
                        values(H - 1)
                if c >= 2:
                    gate_out(c - 2, d_gs)
            with sp.Fori(2, 8) as i:
                t.enter(i, 2, PER_GATE)
                for k in range(2):
                    weights(w_in[0], C_GS + (i * 2 + k) * P, 0)
                    weights(w_in[0], C_GS + (i * 2 + k) * P, 1)
                    gate_out(i * 2 + k - 2, d_gs)
                t.leave(6)

            def gate_in(c, s):
                sp.dma_start(GSI[:, s, :], d_gs[c]).then_inc(S[f"gs_in{s}"], 16)

            def psb_body(c0, first, last):
                for k in range(4):
                    weights(w_sb[0], (c0 + k) * P, 0)
                    if first and k == 1:
                        gate_out(KT - 2, d_gs)
                        gate_out(KT - 1, d_gs)
                        for s in range(2):
                            sp.wait_ge(S[f"sg_out{s}"], 16 * 8)
                        sp.wait_ge(S["lows_done"], 1)
                    if first and k < 1:
                        continue
                    if first and k == 1:
                        gate_in(0, 0)
                        gate_in(1, 1)
                        continue
                    merge_part(c0 + k - 2, k % 2, True)

            def merge_part(c, s, more):
                t.take("m_ready")
                sp.dma_start(d_m[c], MO[:, s, :]).then_inc(S[f"m_out{s}"], 16)
                if more:
                    gate_in(c + 2, s)

            psb_body(0, True, False)
            with sp.Fori(1, 4) as i:
                t.enter(i, 1, PER_PSB)
                psb_body(i * 4, False, False)
                t.leave(3)

            def tables(h):
                t.room("tab_used")
                sp.dma_start(TAB[:], c_tab[h]).then_inc(S["tab_in"], 16)

            def state_pair(h, j, s):
                t.room(f"st_out{s}", 32)
                for k in range(2):
                    sp.dma_start(ST[:, s, k, :], state_ret[0, 2 * j + k, h, :, :]).then_inc(S[f"st_in{s}"], 16)

            def state_pair_out(h, j, s):
                t.take("st_new")
                for k in range(2):
                    sp.dma_start(ret_s[0, 2 * j + k, h, :, :], ST[:, s, k, :]).then_inc(S[f"st_out{s}"], 16)

            def ret_body(h, a, load):
                for p in range(12):
                    load(p)
                    if p == 0 and a is not None:
                        state_pair(a, 0, 0)
                        state_pair(a, 1, 1)
                    if p == 3 and a is not None:
                        t.take("s_ready")
                        sp.dma_start(ret_p[0, 0, a, :, :], SP_[:, 3, :]).then_inc(S["s_out"], 16)
                    if p in (5, 6) and a is not None:
                        state_pair_out(a, p - 5, (p - 5) % 2)
                        state_pair(a, p - 3, (p - 5) % 2)
                    if p in (7, 8) and a is not None:
                        state_pair_out(a, p - 5, (p - 5) % 2)
                    if p == 6 and h is not None:
                        t.room("gain_used")
                        t.settle()
                        sp.dma_start(GN2[:], gn_gain[0, bass.ds(h * DV, DV)].rearrange("(k p) -> p k", p=P),
                                     allow_slow_non_contiguous=True)\
                            .then_inc(S["gain_in"], 16)
                    if p == 9 and h is not None:
                        tables(h)

            def ret_cols(h):
                return [C_RQ + h * P, C_RK + h * P, C_RV + h * DV, C_RV + h * DV + P, C_RG + h * DV,
                        C_RG + h * DV + P]

            for k in range(2):
                weights(w_in[0], ret_cols(0)[0], k)
                merge_part(KT - 2 + k, k, False)
            for s in range(2):
                sp.wait_ge(S[f"m_out{s}"], 16 * 8)
            sp.wait_ge(S["kv_out"], 64 * H)
            sp.dma_start(RCOS[:], c_rope[0]).then_inc(S["rope_in"], 16)
            sp.dma_start(RSIN[:], c_rope[1]).then_inc(S["rope_in"], 16)
            ret_body(0, None, lambda p: p >= 2 and weights(w_in[0], ret_cols(0)[p // 2], p % 2))
            with sp.Fori(1, H) as i:
                t.enter(i, 1, PER_RET)
                ret_body(i, i - 1, lambda p: weights(w_in[0], ret_cols(i)[p // 2], p % 2))
                t.leave(H - 1)

            def gr_load(p):
                weights(w_in[0], C_GR + (p // 2) * P, p % 2)
                if p % 2 and p >= 5:
                    gate_out(p // 2 - 2, d_gr)

            ret_body(None, H - 1, gr_load)
            with sp.Fori(3, 8) as i:
                t.enter(i, 3, PER_GATE)
                for k in range(2):
                    weights(w_in[0], C_GR + (i * 2 + k) * P, 0)
                    weights(w_in[0], C_GR + (i * 2 + k) * P, 1)
                    gate_out(i * 2 + k - 2, d_gr)
                t.leave(5)

            def merge_in(c, s):
                sp.dma_start(MGI[:, s, 0, :], d_gr[c]).then_inc(S[f"mg_in{s}"], 16)
                sp.dma_start(MGI[:, s, 1, :], d_m[c]).then_inc(S[f"mg_in{s}"], 16)

            for k in range(2):
                weights(w_ret[0], 0, k)
                gate_out(KT - 2 + k, d_gr)
            for s in range(2):
                sp.wait_ge(S[f"sg_out{s}"], 16 * 16)
            sp.wait_ge(S["lows_done"], 2)
            merge_in(0, 0)
            merge_in(1, 1)
            weights(w_ret[0], P, 0)
            weights(w_ret[0], P, 1)
            with sp.Fori(1, 8) as i:
                t.enter(i, 1, PER_C)
                for k in range(2):
                    weights(w_ret[0], (i * 2 + k) * P, 0)
                    weights(w_ret[0], (i * 2 + k) * P, 1)
                    t.take("mg_used")
                    merge_in(i * 2 + k, k)
                t.leave(7)

            weights(w_out[0], 0, 0)
            for s in range(2):
                sp.wait_ge(S[f"st_out{s}"], 64 * H)
            sp.wait_ge(S["s_out"], 16 * H)
            sp.dma_start(FG[:], final_gain.rearrange("(o n) -> o n", o=1).broadcast_to([P, D_MODEL]))\
                .then_inc(S["fg_in"], 16)
            weights(w_out[0], 0, 1)
            sp.wait_ge(S["acc_dve1"], 3 * 8)
            sp.dma_start(HH[:, 0:4, :], x_prompt[0].rearrange("(n p) d -> p n d", p=P)).then_inc(S["h_in"], 16)
            sp.dma_start(HH[0:NS, 4, :], x_sample.rearrange("b t n -> (b t) n")).then_inc(S["h_in"], 16)
            weights(w_out[0], P, 0)
            weights(w_out[0], P, 1)
            with sp.Fori(1, 8) as i:
                t.enter(i, 1, PER_D)
                for k in range(2):
                    weights(w_out[0], (i * 2 + k) * P, 0)
                    weights(w_out[0], (i * 2 + k) * P, 1)
                t.leave(7)
            for n in range(4):
                sp.wait_ge(S["y_done"], n + 1)
                sp.dma_start(y_prompt[0, n * P:(n + 1) * P, :], HH[:, n, :]).then_inc(S["y_out"], 16)
            sp.wait_ge(S["y_done"], 5)
            sp.dma_start(y_sample.rearrange("b t n -> (b t) n"), HH[0:NS, 4, :]).then_inc(S["y_out"], 16)
            sp.wait_ge(S["y_out"], 16 * 5)
            sp.wait_ge(S["kv_out"], 64 * H)
            sp.wait_ge(S["s_out"], 16 * H)
            for s in range(2):
                sp.wait_ge(S[f"st_out{s}"], 64 * H)
                sp.wait_ge(S[f"sg_out{s}"], 16 * 16)
                sp.wait_ge(S[f"m_out{s}"], 16 * 8)

        @block.tensor
        def _(pe):
            t = Tally(pe, S)
            slot, group, unsaid = [0], [0], [None]

            def quarter(xh, xl, k0, first, last, to):
                s, a = slot[0] % 4, group[0] % 2
                slot[0] += 1
                if first:
                    t.room(f"acc_read{a}")
                t.take(f"w_full{s}")
                for k in range(QK):
                    for w, x in ((HI, xh), (HI, xl), (LO, xh)):
                        for half in range(2):
                            mm = pe.matmul(ACC[a][:, half, 0:HALF], w[:, s, k, :],
                                           x[:, k0 + k, half * HALF:(half + 1) * HALF],
                                           start=first and k == 0 and w is HI and x is xh,
                                           stop=last and k == QK - 1 and w is LO)
                            if unsaid[0] is not None:
                                mm.then_inc(S[f"w_free{unsaid[0]}"], 1)
                                unsaid[0] = None
                if last:
                    mm.then_inc(S[f"acc_{to}{a}"], 1)
                    group[0] += 1
                    unsaid[0] = s
                else:
                    mm.then_inc(S[f"w_free{s}"], 1)

            def unit(xh, xl, p, to, units=2):
                for q in range(2):
                    quarter(xh, xl, p * 8 + q * 4, p == 0 and q == 0, p == units - 1 and q == 1, to)

            def transpose(out, in_):
                return pe.transpose(out, in_, IDENT[0:in_.shape[0], 0:in_.shape[0]])

            pe.wait_ge(S["consts"], 16)
            for n in range(5):
                rows = P if n < 4 else NS
                pe.wait_ge(S["xs_ready"], n + 1)
                for g in range(4):
                    t.room(f"z_read{g}")
                    for k in range(4):
                        mm = transpose(Z[g][:, k * P:k * P + rows], XN[0:rows, n, (4 * g + k) * P:(4 * g + k + 1) * P])
                    mm.then_inc(S[f"z_dve{g}"], 1)
            pe.wait_ge(S["xh_done"], 20)
            pe.wait_ge(S["xl_done"], 20)

            def cached(b):
                g = b % 2
                t.take(f"k_in{b}", 64)
                t.room(f"z_read{g}")
                for j in range(PAGES):
                    mm = transpose(Z[g][:, j * P:(j + 1) * P], KC[:, b, j * P:(j + 1) * P])
                mm.then_inc(S[f"z_{('act', 'dve')[g]}{g}"], 1)

            def cached_logits(b):
                t.reach(f"z_read{b % 2}")
                for j in range(PAGES):
                    mm = pe.matmul(Z[3][:, j * NS + b * TS:j * NS + (b + 1) * TS], KTR[:, b % 4, j * P:(j + 1) * P],
                                   QS[:, b * TS:(b + 1) * TS], start=True, stop=True)
                return mm

            def suffix(j, col, later):
                o, n = BLK[j]
                mm = pe.matmul(Z[2][:, col:col + n], UPPER, LL[:, o:o + n], start=True, stop=not later)
                for jj in later:
                    oo, m = BLK[jj]
                    mm = pe.matmul(Z[2][:, col + n - m:col + n], ONES, LL[:, oo:oo + m], start=False,
                                   stop=jj == later[-1])
                return mm

            def sb_attention(p):
                if p == 0:
                    t.take("q_ev")
                    t.take("k_ev")
                    for g, blocks in enumerate(((0,), (1,), (2, 3))):
                        t.room(f"z_read{g}")
                        for j in blocks:
                            o, n = BLK[j]
                            c = o - SEG[g][0]
                            mm = pe.matmul(Z[g][:, c:c + n], KTT[:, j * P:(j + 1) * P], QT[:, j * P:SEQ],
                                           start=True, stop=True)
                        mm.then_inc(S[f"z_act{g}"], 1)
                    t.room("z_read3")
                    pe.matmul(Z[3][0:NS, 256:256 + NS], KTT[:, SEQ:T], QT[:, SEQ:T], start=True, stop=True)
                if p == 2:
                    t.take("qs")
                if 2 <= p <= 5:
                    cached_logits(2 * p - 4)
                    mm = cached_logits(2 * p - 3)
                    if p == 5:
                        mm.then_inc(S["z_act3"], 1)
                if 1 <= p <= 4:
                    cached(2 * p - 2)
                    cached(2 * p - 1)
                if p == 2:
                    t.take("l_ready", 3)
                    t.room("z_read2")
                    suffix(0, 0, [1, 2, 3]).then_inc(S["z_dve2"], 1)
                if p == 3:
                    t.room("z_read2")
                    suffix(1, 0, [2, 3]).then_inc(S["z_dve2"], 1)
                if p == 4:
                    t.room("z_read2")
                    suffix(2, 0, [3])
                    suffix(3, 256, []).then_inc(S["z_dve2"], 1)
                if p == 5:
                    t.take("a_ready", 3)
                    t.take("vn", 2)
                    t.room("z_read2")
                    for j, (o, n) in enumerate(BLK):
                        mm = pe.matmul(Z[2][:, SEQ - n:SEQ], VN[:, j, :], ZZ[:, o:o + n], start=j == 0, stop=j == 3)
                    mm.then_inc(S["z_dve2"], 1)
                if p == 6:
                    t.take("l_ready")
                    t.room("z_read3")
                    ln = LL[0:NS, ZN0:ZW]
                    pe.matmul(Z[3][:, 0:256], UPPER, LL[:, ZS0:ZN0], start=True, stop=False)
                    for c in (3, 2, 1):
                        lc = LL[:, ZS0 + c * NS:ZS0 + (c + 1) * NS].rearrange("p (o n) -> p o n", o=1)
                        pe.matmul(Z[3][:, 0:c * NS].rearrange("p (o n) -> p o n", o=c), ONES,
                                  lc.broadcast_to([P, c, NS]), start=False, stop=False)
                    pe.matmul(Z[3][:, 0:256].rearrange("p (o n) -> p o n", o=4), ONES[0:NS, :],
                              ln.rearrange("p (o n) -> p o n", o=1).broadcast_to([NS, 4, NS]), start=False, stop=True)
                    pe.matmul(Z[3][0:NS, 256:256 + NS], UPPER[0:NS, 0:NS], ln, start=True, stop=True)\
                        .then_inc(S["z_dve3"], 1)
                if p == 7:
                    t.take("a_ready")
                    t.room("z_read2")
                    pe.matmul(Z[2][:, 0:NS], VN[0:NS, 4, :], ZZ[0:NS, ZN0:ZW], start=True, stop=False)
                    for b in range(NB):
                        t.take(f"v_in{b}", 64)
                        for j in range(PAGES):
                            mm = pe.matmul(Z[2][:, b * TS:(b + 1) * TS], VC[:, b, j * P:(j + 1) * P],
                                           ZZ[:, ZS0 + j * NS + b * TS:ZS0 + j * NS + (b + 1) * TS],
                                           start=False, stop=b == NB - 1 and j == PAGES - 1)
                    mm.then_inc(S["z_dve2"], 1)

            def sb_new(p):
                if p == 5:
                    t.room("z_read0")
                    for j in range(4):
                        mm = transpose(Z[0][:, j * P:(j + 1) * P], KTT[:, j * P:(j + 1) * P])
                    mm.then_inc(S["z_act0"], 1)
                if p == 6:
                    t.take("v_ev")
                    t.room("z_read2")
                    for j in range(4):
                        mm = transpose(Z[2][:, j * P:(j + 1) * P], VT[:, j * P:(j + 1) * P])
                    mm.then_inc(S["z_dve2"], 1)
                if p == 7:
                    t.room("z_read1")
                    t.settle()
                    transpose(Z[1][0:NS, 0:P], KTT[:, SEQ:T])
                    transpose(Z[1][0:NS, P:2 * P], VT[:, SEQ:T]).then_inc(S["z_dve1"], 1)

            def sb_body(attend):
                for p in range(8):
                    unit(XH, XL, p % 2, "act")
                    if attend:
                        sb_attention(p)
                    if p == 5:
                        pe.wait_ge(S["k_ev"], t.value("k_ev") + 1)
                    sb_new(p)

            sb_body(False)
            with pe.Fori(1, H) as i:
                t.enter(i, 1, PER_SB)
                sb_body(True)
                t.leave(H - 1)
            for p in range(8):
                unit(XH, XL, p % 2, "act")
                sb_attention(p)
            with pe.Fori(2, 8) as i:
                t.enter(i, 2, PER_GATE)
                for p in range(4):
                    unit(XH, XL, p % 2, "act")
                t.leave(6)

            pe.wait_ge(S["lows_done"], 1)
            with pe.Fori(0, 4) as i:
                t.enter(i, 0, PER_PSB)
                for p in range(4):
                    unit(RH, RL, 0, "dve", units=1)
                t.leave(4)

            def ret_attention(p):
                if p == 0:
                    t.take("q_ev")
                    t.take("k_ev")
                    t.room("z_read0")
                    for c in range(4):
                        mm = pe.matmul(Z[0][:, c * P:(c + 1) * P], RKT[:, c * P:(c + 1) * P],
                                       RQT[:, c * P:(c + 1) * P], start=True, stop=True)
                    mm.then_inc(S["z_dve0"], 1)
                    t.room("z_read3")
                    pe.matmul(Z[3][0:NS, 0:NS], RKT[:, SEQ:T], RQT[:, SEQ:T], start=True, stop=True)
                    transpose(Z[3][0:NS, P:2 * P], RKT[:, SEQ:T]).then_inc(S["z_dve3"], 1)
                    t.room("z_read1")
                    for c in range(4):
                        mm = transpose(Z[1][:, c * P:(c + 1) * P], RKT[:, c * P:(c + 1) * P])
                    mm.then_inc(S["z_act1"], 1)
                if p == 1:
                    t.take("kd")
                    t.take("vn", 4)
                    for g, cc in ((1, (0, 1)), (2, (2, 3))):
                        t.room(f"z_read{g}")
                        for c in cc:
                            mm = pe.matmul(Z[g][:, (c % 2) * DV:(c % 2 + 1) * DV], KD[:, c, :], RVN[:, c, :],
                                           start=True, stop=True)
                        mm.then_inc(S[f"z_dve{g}"], 1)
                if p in (2, 3):
                    g = p - 2
                    if p == 2:
                        t.take("p_ready", 2)
                        t.take("qd")
                        t.take("s_ready")
                    t.room(f"z_read{g}")
                    for c in (2 * g, 2 * g + 1):
                        o = Z[g][:, (c % 2) * DV:(c % 2 + 1) * DV]
                        mm = pe.matmul(o, PR[:, c, :], RVN[:, c, :], start=True, stop=c == 0)
                        if c:
                            mm = pe.matmul(o, QD[:, c - 1, :], SP_[:, c - 1, :], start=False, stop=True)
                    mm.then_inc(S[f"z_dve{g}"], 1)
                if p == 2:
                    t.take("km")
                    t.room("z_read3")
                    t.settle()
                    pe.matmul(Z[3][0:NS, 0:DV], PS[:, :], RVN[0:NS, 4, :], start=True, stop=False)
                if 2 <= p <= 5:
                    j, s = p - 2, p % 2
                    t.take(f"st_in{s}", 32)
                    for k in range(2):
                        mm = pe.matmul(Z[3][0:NS, 0:DV], QM[:, 2 * j + k, :], ST[:, s, k, :], start=False,
                                       stop=j == 3 and k == 1)
                    if p == 5:
                        mm.then_inc(S["z_dve3"], 1)
                    t.room("z_read2")
                    for k in range(2):
                        mm = pe.matmul(Z[2][:, k * DV:(k + 1) * DV], KM[:, 2 * j + k, :], RVN[0:NS, 4, :],
                                       start=True, stop=True)
                    mm.then_inc(S["z_dve2"], 1)
                if p in (5, 6):
                    g = p - 5
                    if p == 5:
                        t.take("on", 4)
                    t.room(f"z_read{g}")
                    for c in range(4):
                        mm = transpose(Z[g][:, c * P:(c + 1) * P], ON[:, c, g * P:(g + 1) * P])
                    mm.then_inc(S[f"z_dve{g}"], 1)

            def ret_new(p):
                if p in (6, 8):
                    t.take("v_ev")
                    t.room("z_read2")
                    for c in range(4):
                        mm = transpose(Z[2][:, c * P:(c + 1) * P], RVT[:, c * P:(c + 1) * P])
                    mm.then_inc(S["z_act2"], 1)

            def ret_body(attend, new):
                for p in range(12):
                    unit(XH, XL, p % 2, "dve" if new and p < 4 else "act")
                    if attend:
                        ret_attention(p)
                    if new:
                        ret_new(p)
                    if p == 7:
                        t.room("z_read3")
                        if attend:
                            t.take("on")
                            t.settle()
                            for g in range(2):
                                mm = transpose(Z[3][:, g * NS:(g + 1) * NS], ON[0:NS, 4, g * P:(g + 1) * P])
                        if new:
                            if not attend:
                                t.settle()
                            mm = transpose(Z[3][0:NS, 256:256 + P], RVT[:, SEQ:T])
                        mm.then_inc(S["z_dve3"], 1)
                    if p == 9 and new:
                        t.room("z_read3")
                        t.settle()
                        transpose(Z[3][0:NS, 256:256 + P], RVT[:, SEQ:T]).then_inc(S["z_dve3"], 1)

            ret_body(False, True)
            with pe.Fori(1, H) as i:
                t.enter(i, 1, PER_RET)
                ret_body(True, True)
                t.leave(H - 1)
            ret_body(True, False)
            with pe.Fori(3, 8) as i:
                t.enter(i, 3, PER_GATE)
                for p in range(4):
                    unit(XH, XL, p % 2, "act")
                t.leave(5)

            pe.wait_ge(S["lows_done"], 2)
            with pe.Fori(0, 8) as i:
                t.enter(i, 0, PER_C)
                for p in range(4):
                    unit(RH, RL, p % 2, "dve")
                t.leave(8)

            def back(k):
                t.take("y_ev")
                t.room(f"z_read{k}")
                for n in range(4):
                    mm = transpose(Z[k][:, n * P:(n + 1) * P], YT[:, k, n * P:(n + 1) * P])
                mm.then_inc(S[f"z_dve{k}"], 1)
                t.room(f"z_read{2 + k}")
                t.settle()
                transpose(Z[2 + k][0:NS, 0:P], YT[:, k, SEQ:T]).then_inc(S[f"z_dve{2 + k}"], 1)

            pe.wait_ge(S["lows_done"], 3)
            for p in range(4):
                unit(XH, XL, p % 2, "act")
                if p == 2:
                    back(0)
            with pe.Fori(1, 8) as i:
                t.enter(i, 1, PER_D)
                for p in range(4):
                    unit(XH, XL, p % 2, "act")
                    if p == 0:
                        back(1)
                    if p == 2:
                        back(0)
                t.leave(7)
            back(1)

        @block.scalar
        def _(act):
            t = Tally(act, S)
            splits = [0]

            def split():
                n = splits[0]
                splits[0] += 1
                s, r = n % 4, n // 2 % 2
                if n % 2 == 0:
                    t.take(f"raw_in{r}", 16)
                t.room(f"w_free{s}")
                act.activation(HI[:, s], RAW[:, r, (n % 2) * QK:(n % 2 + 1) * QK, :], ACT.Copy)\
                    .then_inc(S[f"hi_full{s}"], 1)

            act.preload_act_table_set("natural_log_exp_and_others")
            for n in range(5):
                rows = P if n < 4 else NS
                act.wait_ge(S[f"x_in{n}"], 16)
                act.activation(JUNK[0:rows, :], XN[0:rows, n, :], ACT.Square, accum_out=SSQ[0:rows, n:n + 1])
                act.drain()
                act.activation(RSTD[0:rows, n:n + 1], SSQ[0:rows, n:n + 1], ACT.Ln, scale=1.0 / D_MODEL,
                               bias=EPS_RMS)
                act.drain()
                act.activation(RSTD[0:rows, n:n + 1], RSTD[0:rows, n:n + 1], ACT.Exp, scale=-0.5)\
                    .then_inc(S["rs0"], 1)
            for u in range(20):
                n, g = u // 4, u % 4
                rows = P if n < 4 else NS
                act.wait_ge(S["x_t"], u + 1)
                act.activation(XH[:, 4 * g:4 * g + 4, n * P:n * P + rows], XT[:, u % 2, :, 0:rows], ACT.Copy)\
                    .then_inc(S["xh_done"], 1)
            act.wait_ge(S["vecs"], 32)
            for _ in range(3):
                split()

            def evacuate(s, dst, ev):
                t.take(f"acc_act{s}")
                act.activation(two(dst[:, :]), acc(s), ACT.Copy).then_inc(S[ev], 1)

            def softplus_tail(lo, hi, parts):
                t.take("w_abs", parts)
                act.activation(LL[:, lo:hi], LL[:, lo:hi], ACT.Exp)
                act.drain()
                act.activation(LL[:, lo:hi], LL[:, lo:hi], ACT.Ln, bias=1.0).then_inc(S["w_ln"], parts)

            def sb_attention(p, a):
                if p == 0:
                    act.activation(BIAS[:, 0:1], SBB[:, bass.ds(a, 1)], ACT.Copy)
                    act.drain()
                    for g, (o, n) in enumerate(SEG):
                        t.take(f"z_act{g}")
                        act.activation(ZZ[:, o:o + n], Z[g][:, 0:n], ACT.Identity, scale=SCALE, bias=BIAS[:, 0:1])\
                            .then_inc(S["zs_ready"], 1)
                        act.drain().then_inc(S[f"z_read{g}"], 1)
                    act.activation(QS[:, :], QT[:, SEQ:T], ACT.Copy).then_inc(S["qs"], 1)
                    softplus_tail(0, ZS0, 3)
                if 1 <= p <= 4:
                    b = 2 * p - 2
                    t.take("z_act0")
                    act.activation(KTR[:, b % 4, :], Z[0][:, :], ACT.Copy)\
                        .then_inc(S["z_read0"], 1)
                if 3 <= p <= 5:
                    o, n = SEG[p - 3]
                    t.take("x_ready")
                    act.activation(ZZ[:, o:o + n], ZZ[:, o:o + n], ACT.Exp).then_inc(S["a_ready"], 1)
                if p == 5:
                    t.take("z_act3")
                    act.activation(ZZ[:, ZS0:ZN0], Z[3][:, 0:256], ACT.Identity, scale=SCALE, bias=BIAS[:, 0:1])
                    act.activation(ZZ[0:NS, ZN0:ZW], Z[3][0:NS, 256:256 + NS], ACT.Identity, scale=SCALE,
                                   bias=BIAS[0:NS, 0:1]).then_inc(S["zs_ready"], 1)
                    act.drain().then_inc(S["z_read3"], 1)
                    softplus_tail(ZS0, ZW, 1)
                if p == 6:
                    t.take("t_ready")
                    act.activation(RH[:, bass.ds(a, 1), 0:SEQ], TT[:, 0:SEQ].rearrange("p (o n) -> p o n", o=1), ACT.Copy)\
                        .then_inc(S["rh_done"], 1)
                    t.take("x_ready")
                    act.activation(ZZ[:, ZS0:ZN0], ZZ[:, ZS0:ZN0], ACT.Exp)
                    act.activation(ZZ[0:NS, ZN0:ZW], ZZ[0:NS, ZN0:ZW], ACT.Exp).then_inc(S["a_ready"], 1)
                if p == 7:
                    t.take("t_ready")
                    act.activation(RH[:, bass.ds(a, 1), SEQ:T], TT[:, SEQ:T].rearrange("p (o n) -> p o n", o=1), ACT.Copy)\
                        .then_inc(S["rh_done"], 1)

            def gate_exp(s, dst):
                t.take(f"acc_act{s}")
                act.activation(two(dst), acc(s), ACT.Exp, scale=-1.0).then_inc(S["ge"], 1)

            def sb_new(p):
                if p == 1:
                    evacuate(0, QT, "q_ev")
                    act.drain().then_inc(S["acc_read0"], 1)
                if p == 3:
                    evacuate(1, KTT, "k_ev")
                    act.drain().then_inc(S["acc_read1"], 1)
                if p == 5:
                    evacuate(0, VT, "v_ev")
                    act.drain().then_inc(S["acc_read0"], 1)
                    t.room("kv_out", 64)
                    t.take("z_act0")
                    act.activation(KN[:, 0:4, :], Z[0][:, :].rearrange("p (n d) -> p n d", n=4), ACT.Copy)\
                        .then_inc(S["z_read0"], 1)
                if p == 7:
                    gate_exp(1, GT[:, :])

            def sb_body(a):
                for p in range(8):
                    split()
                    split()
                    if a is not None:
                        sb_attention(p, a)
                    sb_new(p)

            sb_body(None)
            with act.Fori(1, H) as i:
                t.enter(i, 1, PER_SB)
                sb_body(i - 1)
                t.leave(H - 1)

            gate_n = [0]

            def gate(dst):
                s = gate_n[0] % 2
                gate_n[0] += 1
                t.room(f"sg_out{s}", 16)
                gate_exp(s, dst[:, s, :])
                act.drain().then_inc(S[f"acc_read{s}"], 1)

            for p in range(8):
                split()
                split()
                sb_attention(p, H - 1)
                if p % 2:
                    gate(SG)
            with act.Fori(2, 8) as i:
                t.enter(i, 2, PER_GATE)
                for p in range(4):
                    split()
                    split()
                    if p % 2:
                        gate(SG)
                t.leave(6)
            with act.Fori(0, 4) as i:
                t.enter(i, 0, PER_PSB)
                for p in range(8):
                    split()
                t.leave(4)

            def ret_attention(p, a):
                if p == 0:
                    t.take("tab_in", 16)
                    t.take("z_act1")
                    act.activation(KD[:, :, :], Z[1][:, :].rearrange("p (n d) -> p n d", n=4), ACT.Copy,
                                   scale=TAB[:, T_KP:T_KP + 1]).then_inc(S["kd"], 1)
                    act.drain().then_inc(S["z_read1"], 1)
                if p in (3, 4, 6):
                    for c in {3: (0, 1), 4: (2, 3), 6: (4,)}[p]:
                        rows = P if c < 4 else NS
                        t.take("stat")
                        act.activation(RS5[0:rows, c:c + 1], MV[0:rows, c, 1:2], ACT.Ln, bias=EPS_GN)
                        act.drain()
                        act.activation(RS5[0:rows, c:c + 1], RS5[0:rows, c:c + 1], ACT.Exp, scale=-0.5)\
                            .then_inc(S["rstd"], 1)
                if p in (6, 7):
                    g = p - 6
                    t.take("t_ready")
                    act.activation(RH[:, bass.ds(a * 2 + g, 1), 0:SEQ], RT[:, 0:SEQ].rearrange("p (o n) -> p o n", o=1),
                                   ACT.Copy).then_inc(S["rh_done"], 1)
                if p == 8:
                    for g in range(2):
                        t.take("t_ready")
                        act.activation(RH[:, bass.ds(a * 2 + g, 1), SEQ:T],
                                       RT[:, g * NS:(g + 1) * NS].rearrange("p (o n) -> p o n", o=1), ACT.Copy)\
                            .then_inc(S["rh_done"], 1)

            def ret_new(p, attend):
                if p in (5, 7):
                    s = 0 if p == 5 else 1
                    if p == 7:
                        t.take("z_dve3", 3 if attend else 1)
                    evacuate(s, RVT, "v_ev")
                    act.drain().then_inc(S[f"acc_read{s}"], 1)
                if p in (7, 9):
                    g = 0 if p == 7 else 1
                    t.take("z_act2")
                    act.activation(RVN[:, 0:4, g * P:(g + 1) * P], Z[2][:, :].rearrange("p (n d) -> p n d", n=4),
                                   ACT.Copy).then_inc(S["vn"], 1)
                    act.drain().then_inc(S["z_read2"], 1)
                if p == 9:
                    t.skip("z_dve3")
                if p in (9, 11):
                    t.room("rgt_read")
                    gate_exp(0 if p == 9 else 1, RGT[:, :])

            def ret_body(a, new):
                for p in range(12):
                    split()
                    split()
                    if a is not None:
                        ret_attention(p, a)
                    if new:
                        ret_new(p, a is not None)
                    elif p % 2:
                        gate(SG2)

            act.wait_ge(S["rope_in"], 32)
            t.n["z_dve3"] = 5 + H
            ret_body(None, True)
            with act.Fori(1, H) as i:
                t.enter(i, 1, PER_RET)
                ret_body(i - 1, True)
                t.leave(H - 1)
            ret_body(H - 1, False)
            with act.Fori(3, 8) as i:
                t.enter(i, 3, PER_GATE)
                for p in range(4):
                    split()
                    split()
                    if p % 2:
                        gate(SG2)
                t.leave(5)

            with act.Fori(0, 8) as i:
                t.enter(i, 0, PER_C)
                for p in range(4):
                    split()
                    split()
                    if p % 2:
                        t.take("t_ready")
                        act.activation(XH[:, bass.ds(i * 2 + p // 2, 1), :],
                                       MT[:, :].rearrange("p (o n) -> p o n", o=1), ACT.Copy)\
                            .then_inc(S["rh_done"], 1)
                t.leave(8)

            def out_body(last):
                for p in range(4):
                    for q in range(2):
                        if not (last and 2 * p + q >= 5):
                            split()
                    if p % 2:
                        s = p // 2
                        t.take(f"acc_act{s}")
                        act.activation(two(YT[:, s, :]), acc(s), ACT.Copy).then_inc(S["y_ev"], 1)
                        act.drain().then_inc(S[f"acc_read{s}"], 1)

            with act.Fori(0, 7) as i:
                t.enter(i, 0, PER_D)
                out_body(False)
                t.leave(7)
            out_body(True)
            act.wait_ge(S["fg_in"], 16)
            act.wait_ge(S["lows_done"], 4)
            for n in range(5):
                rows = P if n < 4 else NS
                act.activation(JF[0:rows, :], HH[0:rows, n, :], ACT.Square, accum_out=SSQ[0:rows, n:n + 1])
                act.drain()
                act.activation(RSTD[0:rows, n:n + 1], SSQ[0:rows, n:n + 1], ACT.Ln, scale=1.0 / D_MODEL,
                               bias=EPS_RMS)
                act.drain()
                act.activation(RSTD[0:rows, n:n + 1], RSTD[0:rows, n:n + 1], ACT.Exp, scale=-0.5)\
                    .then_inc(S["rs_f"], 1)

        @block.vector
        def _(dve):
            t = Tally(dve, S)
            splits = [0]

            def split():
                n = splits[0]
                splits[0] += 1
                s, r = n % 4, n // 2 % 2
                t.take(f"hi_full{s}")
                dve.tensor_tensor(LO[:, s], RAW[:, r, (n % 2) * QK:(n % 2 + 1) * QK, :], HI[:, s].bitcast(F32),
                                  ALU.subtract).then_inc(S[f"w_full{s}"], 1)
                if n % 2:
                    dve.drain().then_inc(S[f"raw_free{r}"], 1)

            dve.wait_ge(S["vecs"], 32)
            for n in range(5):
                rows = P if n < 4 else NS
                dve.wait_ge(S["rs0"], n + 1)
                dve.tensor_scalar(XN[0:rows, n, :], XN[0:rows, n, :], RSTD[0:rows, n:n + 1], None, ALU.mult)\
                    .then_inc(S["xs_ready"], 1)
            for u in range(21):
                if u < 20:
                    n, g = u // 4, u % 4
                    rows = P if n < 4 else NS
                    t.take(f"z_dve{g}")
                    dve.tensor_tensor(XT[:, u % 2, :, 0:rows],
                                      Z[g][:, :].rearrange("p (k n) -> p k n", k=4)[:, :, 0:rows],
                                      NG[:, 4 * g:4 * g + 4].rearrange("p (k o) -> p k o", o=1)
                                      .broadcast_to([P, 4, rows]), ALU.mult).then_inc(S["x_t"], 1)
                    dve.drain().then_inc(S[f"z_read{g}"], 1)
                if u:
                    v = u - 1
                    n, g = v // 4, v % 4
                    rows = P if n < 4 else NS
                    dve.wait_ge(S["xh_done"], v + 1)
                    xc = slice(n * P, n * P + rows)
                    dve.tensor_tensor(XL[:, 4 * g:4 * g + 4, xc], XT[:, v % 2, :, 0:rows],
                                      XH[:, 4 * g:4 * g + 4, xc].bitcast(F32), ALU.subtract)\
                        .then_inc(S["xl_done"], 1)
                    dve.drain()
            dve.memset(ZZ[:, ZN0:ZW], 0.0)
            for _ in range(3):
                split()

            def negative_abs(lo, hi):
                t.take("zs_ready")
                dve.scalar_tensor_tensor(LL[:, lo:hi], ZZ[:, lo:hi], -1.0, ZZ[:, lo:hi], ALU.mult, ALU.min)\
                    .then_inc(S["w_abs"], 1)

            def log_keep(lo, hi):
                t.take("w_ln")
                dve.scalar_tensor_tensor(LL[:, lo:hi], ZZ[:, lo:hi], 0.0, LL[:, lo:hi], ALU.max, ALU.add)\
                    .then_inc(S["l_raw"], 1)

            def low(dst, src, hi):
                t.take("rh_done")
                dve.tensor_tensor(dst, src, hi.bitcast(F32), ALU.subtract)

            def one(ap):
                return ap.rearrange("p (o n) -> p o n", o=1)

            def sb_attention(p, a):
                if p == 0:
                    for o, n in SEG:
                        negative_abs(o, o + n)
                    for o, n in SEG:
                        log_keep(o, o + n)
                if 1 <= p <= 4:
                    b = 2 * p - 1
                    t.take("z_dve1")
                    dve.tensor_copy(KTR[:, b % 4, :], Z[1][:, :]).then_inc(S["z_read1"], 1)
                if 2 <= p <= 4:
                    o, n = SEG[p - 2]
                    t.take("z_dve2")
                    dve.tensor_tensor(ZZ[:, o:o + n], ZZ[:, o:o + n], Z[2][:, 0:n], ALU.subtract)\
                        .then_inc(S["x_raw"], 1)
                    dve.drain().then_inc(S["z_read2"], 1)
                if p == 5:
                    t.take("z_dve2")
                    dve.tensor_tensor(TT[:, 0:SEQ], Z[2][:, :], GG[:, 0:SEQ], ALU.mult).then_inc(S["t_ready"], 1)
                    dve.drain().then_inc(S["z_read2"], 1)
                    negative_abs(ZS0, ZW)
                    log_keep(ZS0, ZW)
                if p == 6:
                    low(RL[:, bass.ds(a, 1), 0:SEQ], one(TT[:, 0:SEQ]), RH[:, bass.ds(a, 1), 0:SEQ])
                    t.take("z_dve3")
                    dve.tensor_tensor(ZZ[:, ZS0:ZN0], ZZ[:, ZS0:ZN0], Z[3][:, 0:256], ALU.subtract)
                    dve.tensor_tensor(ZZ[0:NS, ZN0:ZW], ZZ[0:NS, ZN0:ZW], Z[3][0:NS, 256:256 + NS], ALU.subtract)\
                        .then_inc(S["x_raw"], 1)
                    dve.drain().then_inc(S["z_read3"], 1)
                if p == 7:
                    t.take("z_dve2")
                    dve.tensor_tensor(TT[:, SEQ:T], Z[2][:, 0:NS], GG[:, SEQ:T], ALU.mult).then_inc(S["t_ready"], 1)
                    dve.drain().then_inc(S["z_read2"], 1)
                    low(RL[:, bass.ds(a, 1), SEQ:T], one(TT[:, SEQ:T]), RH[:, bass.ds(a, 1), SEQ:T])

            def sigmoid(buf):
                t.take("ge")
                dve.tensor_scalar(buf, buf, BIG, 1.0, ALU.min, ALU.add)
                dve.drain()
                ins = dve.reciprocal(buf, buf)
                return ins

            def sb_new(p):
                if p == 6:
                    t.room("kv_out", 64)
                    t.take("z_dve2")
                    dve.tensor_copy(VN[:, 0:4, :], Z[2][:, :].rearrange("p (n d) -> p n d", n=4))\
                        .then_inc(S["vn"], 1)
                    dve.drain().then_inc(S["z_read2"], 1)
                if p == 7:
                    t.take("z_dve1")
                    dve.tensor_copy(KN[0:NS, 4, :], Z[1][0:NS, 0:P])
                    dve.tensor_copy(VN[0:NS, 4, :], Z[1][0:NS, P:2 * P]).then_inc(S["vn"], 1)
                    dve.drain().then_inc(S["z_read1"], 1)
                    sigmoid(GT[:, :])
                    dve.drain()
                    dve.tensor_tensor(two(GG[:, :]), acc(1), two(GT[:, :]), ALU.mult)
                    dve.drain().then_inc(S["acc_read1"], 1)

            def sb_body(a):
                for p in range(8):
                    split()
                    split()
                    if a is not None:
                        sb_attention(p, a)
                    sb_new(p)

            sb_body(None)
            with dve.Fori(1, H) as i:
                t.enter(i, 1, PER_SB)
                sb_body(i - 1)
                t.leave(H - 1)

            gate_n = [0]

            def gate(dst):
                s = gate_n[0] % 2
                gate_n[0] += 1
                sigmoid(dst[:, s, :]).then_inc(S["sg_ready"], 1)

            for p in range(8):
                split()
                split()
                sb_attention(p, H - 1)
                if p % 2:
                    gate(SG)
            dve.drain().then_inc(S["lows_done"], 1)
            with dve.Fori(2, 8) as i:
                t.enter(i, 2, PER_GATE)
                for p in range(4):
                    split()
                    split()
                    if p % 2:
                        gate(SG)
                t.leave(6)

            with dve.Fori(0, 4) as i:
                t.enter(i, 0, PER_PSB)
                for p in range(4):
                    split()
                    split()
                    s = p % 2
                    t.take(f"gs_in{s}", 16)
                    t.room(f"m_out{s}", 16)
                    t.take(f"acc_dve{s}")
                    dve.tensor_tensor(two(MO[:, s, :]), acc(s), two(GSI[:, s, :]), ALU.mult)
                    dve.drain().then_inc(S[f"acc_read{s}"], 1)
                    dve.drain().then_inc(S["m_ready"], 1)
                t.leave(4)

            def rotary(s, dst, ev):
                t.take(f"acc_dve{s}")
                for lo, hi in ((0, 64), (64, 128)):
                    dve.tensor_tensor(two(RT[hi % 128:hi % 128 + 64, :]), ACC[s][lo:hi, :, 0:HALF],
                                      two(RSIN[lo:hi, :]), ALU.mult)
                dve.tensor_tensor(two(dst[:, :]), acc(s), two(RCOS[:, :]), ALU.mult)
                dve.drain().then_inc(S[f"acc_read{s}"], 1)
                dve.tensor_tensor(dst[:, :], dst[:, :], RT[:, :], ALU.add).then_inc(S[ev], 1)

            def normalise(c, zb, col):
                rows = P if c < 4 else NS
                dve.bn_stats(STAT[0:rows, c, :], zb[0:rows, col:col + DV])
                dve.drain()
                dve.bn_aggr(MV[0:rows, c, :], STAT[0:rows, c, :]).then_inc(S["stat"], 1)

            def apply_norm(c, zb, col):
                rows = P if c < 4 else NS
                t.take("rstd")
                return dve.tensor_scalar(ON[0:rows, c, :], zb[0:rows, col:col + DV], MV[0:rows, c, 0:1],
                                         RS5[0:rows, c:c + 1], ALU.subtract, ALU.mult).then_inc(S["on"], 1)

            def ret_attention(p, a):
                if p == 0:
                    t.take("tab_in", 16)
                    t.take("z_dve0")
                    dve.tensor_tensor(PR[:, :, :], Z[0][:, :].rearrange("p (c n) -> p c n", c=4),
                                      one(TAB[:, T_DP:T_DP + P]).broadcast_to([P, 4, P]), ALU.mult)\
                        .then_inc(S["p_ready"], 1)
                    dve.drain().then_inc(S["z_read0"], 1)
                    t.take("z_dve3")
                    dve.tensor_tensor(PS[:, :], Z[3][0:NS, 0:NS], TAB[0:NS, T_DS:T_DS + NS], ALU.mult)\
                        .then_inc(S["p_ready"], 1)
                    dve.tensor_tensor(KM[:, :, :], one(Z[3][0:NS, P:2 * P]).broadcast_to([NS, NB, P]),
                                      TAB[0:NS, T_KS:T_KS + NB].rearrange("p (b o) -> p b o", o=1)
                                      .broadcast_to([NS, NB, P]), ALU.mult).then_inc(S["km"], 1)
                    dve.drain().then_inc(S["z_read3"], 1)
                if p == 1:
                    t.room("s_out", 16)
                    t.take("z_dve1")
                    dve.tensor_copy(SP_[:, 0, :], Z[1][:, 0:DV])
                    dve.drain()
                    dve.scalar_tensor_tensor(SP_[:, 1, :], SP_[:, 0, :], TAB[:, T_GC:T_GC + 1], Z[1][:, DV:2 * DV],
                                             ALU.mult, ALU.add)
                    dve.drain().then_inc(S["z_read1"], 1)
                    t.take("z_dve2")
                    dve.scalar_tensor_tensor(SP_[:, 2, :], SP_[:, 1, :], TAB[:, T_GC:T_GC + 1], Z[2][:, 0:DV],
                                             ALU.mult, ALU.add)
                    dve.drain()
                    dve.scalar_tensor_tensor(SP_[:, 3, :], SP_[:, 2, :], TAB[:, T_GC:T_GC + 1], Z[2][:, DV:2 * DV],
                                             ALU.mult, ALU.add).then_inc(S["s_ready"], 1)
                    dve.drain().then_inc(S["z_read2"], 1)
                if 2 <= p <= 5:
                    s = p % 2
                    t.take("z_dve2")
                    dve.scalar_tensor_tensor(ST[:, s, :, :], ST[:, s, :, :], TAB[:, T_G8:T_G8 + 1],
                                             Z[2][:, :].rearrange("p (k e) -> p k e", k=2), ALU.mult, ALU.add)\
                        .then_inc(S["st_new"], 1)
                    dve.drain().then_inc(S["z_read2"], 1)
                    if p == 5:
                        dve.drain().then_inc(S["tab_used"], 1)
                if p in (2, 3):
                    g = p - 2
                    t.take(f"z_dve{g}")
                    for c in (2 * g, 2 * g + 1):
                        normalise(c, Z[g], (c % 2) * DV)
                if p in (3, 4):
                    g = p - 3
                    for c in (2 * g, 2 * g + 1):
                        apply_norm(c, Z[g], (c % 2) * DV)
                    dve.drain().then_inc(S[f"z_read{g}"], 1)
                if p == 5:
                    t.take("z_dve3")
                    normalise(4, Z[3], 0)
                if p == 6:
                    apply_norm(4, Z[3], 0)
                    dve.drain().then_inc(S["z_read3"], 1)
                if p in (5, 6):
                    g = p - 5
                    t.take(f"z_dve{g}")
                    dve.tensor_tensor(RT[:, 0:SEQ], Z[g][:, :], RG[:, g, 0:SEQ], ALU.mult).then_inc(S["t_ready"], 1)
                    dve.drain().then_inc(S[f"z_read{g}"], 1)

            def ret_low(g, a):
                low(RL[:, bass.ds(a * 2 + g, 1), 0:SEQ], one(RT[:, 0:SEQ]), RH[:, bass.ds(a * 2 + g, 1), 0:SEQ])
                dve.drain()

            def ret_tail(p, a, new):
                if p == 7:
                    t.take("z_dve3")
                    if new:
                        dve.tensor_copy(RVN[0:NS, 4, 0:P], Z[3][0:NS, 256:256 + P]).then_inc(S["vn"], 1)
                    if a is not None:
                        for g in range(2):
                            dve.tensor_tensor(RT[:, g * NS:(g + 1) * NS], Z[3][:, g * NS:(g + 1) * NS],
                                              RG[:, g, SEQ:T], ALU.mult).then_inc(S["t_ready"], 1)
                    dve.drain().then_inc(S["z_read3"], 1)
                if p == 8 and a is not None:
                    for g in range(2):
                        low(RL[:, bass.ds(a * 2 + g, 1), SEQ:T], one(RT[:, g * NS:(g + 1) * NS]),
                            RH[:, bass.ds(a * 2 + g, 1), SEQ:T])
                    dve.drain()
                if p == 9 and new:
                    t.take("z_dve3")
                    dve.tensor_copy(RVN[0:NS, 4, P:2 * P], Z[3][0:NS, 256:256 + P]).then_inc(S["vn"], 1)
                    dve.drain().then_inc(S["z_read3"], 1)

            def ret_new(p, attend):
                if p == 1:
                    if attend:
                        t.take("qd")
                    rotary(0, RQT, "q_ev")
                if p == 3:
                    rotary(1, RKT, "k_ev")
                if p in (9, 11):
                    s = 0 if p == 9 else 1
                    if p == 9:
                        t.take("gain_in", 16)
                    sigmoid(RGT[:, :])
                    dve.drain()
                    dve.scalar_tensor_tensor(two(RG[:, s, :]), acc(s), GN2[:, s:s + 1], two(RGT[:, :]),
                                             ALU.mult, ALU.mult)
                    dve.drain().then_inc(S[f"acc_read{s}"], 1)
                    dve.drain().then_inc(S["rgt_read"], 1)
                    if p == 11:
                        dve.drain().then_inc(S["gain_used"], 1)

            def ret_body(a, new):
                for p in range(12):
                    split()
                    split()
                    if a is not None:
                        if p in (6, 7):
                            ret_low(p - 6, a)
                        ret_attention(p, a)
                    ret_tail(p, a, new)
                    if new:
                        ret_new(p, a is not None)
                    elif p % 2:
                        gate(SG2)

            dve.wait_ge(S["rope_in"], 32)
            ret_body(None, True)
            with dve.Fori(1, H) as i:
                t.enter(i, 1, PER_RET)
                ret_body(i - 1, True)
                t.leave(H - 1)
            ret_body(H - 1, False)
            dve.drain().then_inc(S["lows_done"], 1)
            with dve.Fori(3, 8) as i:
                t.enter(i, 3, PER_GATE)
                for p in range(4):
                    split()
                    split()
                    if p % 2:
                        gate(SG2)
                t.leave(5)

            with dve.Fori(0, 8) as i:
                t.enter(i, 0, PER_C)
                for p in range(4):
                    split()
                    split()
                    if p % 2:
                        s = p // 2
                        c = i * 2 + s
                        t.take(f"mg_in{s}", 32)
                        t.take(f"acc_dve{s}")
                        dve.tensor_tensor(two(MT[:, :]), acc(s), two(MGI[:, s, 0, :]), ALU.mult)
                        dve.drain().then_inc(S[f"acc_read{s}"], 1)
                        dve.tensor_tensor(MT[:, :], MT[:, :], MGI[:, s, 1, :], ALU.add).then_inc(S["t_ready"], 1)
                        dve.drain().then_inc(S["mg_used"], 1)
                        low(XL[:, bass.ds(c, 1), :], one(MT[:, :]), XH[:, bass.ds(c, 1), :])
                        dve.drain()
                t.leave(8)
            dve.drain().then_inc(S["lows_done"], 1)

            def add(c, s):
                t.take(f"z_dve{s}")
                cols = HH[:, 0:4, bass.ds(c * P, P)]
                dve.tensor_tensor(cols, cols, Z[s][:, :].rearrange("p (n d) -> p n d", n=4), ALU.add)
                dve.drain().then_inc(S[f"z_read{s}"], 1)
                t.take(f"z_dve{2 + s}")
                cols = HH[0:NS, 4, bass.ds(c * P, P)]
                dve.tensor_tensor(cols, cols, Z[2 + s][0:NS, 0:P], ALU.add)
                dve.drain().then_inc(S[f"z_read{2 + s}"], 1)

            def out_body(i, first, last):
                for p in range(4):
                    for q in range(2):
                        if not (last and 2 * p + q >= 5):
                            split()
                    if p == 0 and not first:
                        add(i * 2 - 1, 1)
                    if p == 2:
                        if first:
                            dve.wait_ge(S["h_in"], 32)
                        add(i * 2, 0)

            out_body(0, True, False)
            with dve.Fori(1, 7) as i:
                t.enter(i, 1, PER_D)
                out_body(i, False, False)
                t.leave(6)
            out_body(7, False, True)
            add(KT - 1, 1)
            dve.drain().then_inc(S["lows_done"], 1)
            dve.wait_ge(S["fg_in"], 16)
            for n in range(5):
                rows = P if n < 4 else NS
                dve.wait_ge(S["rs_f"], n + 1)
                dve.scalar_tensor_tensor(HH[0:rows, n, :], HH[0:rows, n, :], RSTD[0:rows, n:n + 1], FG[0:rows, :],
                                         ALU.mult, ALU.mult).then_inc(S["y_done"], 1)

        @block.gpsimd
        def _(pool):
            t = Tally(pool, S)

            def causal(buf, o, fill):
                blk = buf[:, o:o + P]
                return pool.affine_select(out=blk, in_=blk, compare_op=ALU.is_gt, fill=fill, base=0,
                                          pattern=[[1, P]], channel_multiplier=-1)

            def causal_new(buf, fill):
                blk = buf[0:NS, ZN0:ZW]
                pool.affine_select(out=blk, in_=blk, compare_op=ALU.is_gt, fill=fill, base=0,
                                   pattern=[[1, NS]], channel_multiplier=-1)
                pool.drain()
                blk = blk.rearrange("p (b t) -> p b t", b=NB)
                return pool.affine_select(out=blk, in_=blk, compare_op=ALU.is_ge, fill=fill, base=0,
                                          pattern=[[-TS, NB], [0, TS]], channel_multiplier=1)

            def mask(buf, fill, raw, ready, g):
                t.take(raw)
                t.settle()
                for o in ((0,), (512,), (896, 1152))[g]:
                    ins = causal(buf, o, fill)
                ins.then_inc(S[ready], 1)

            def sb_attention():
                for g in range(3):
                    mask(LL, 0.0, "l_raw", "l_ready", g)
                for g in range(3):
                    mask(ZZ, NO, "x_raw", "x_ready", g)
                t.take("l_raw")
                t.settle()
                causal_new(LL, 0.0).then_inc(S["l_ready"], 1)
                t.take("x_raw")
                t.settle()
                causal_new(ZZ, NO).then_inc(S["x_ready"], 1)

            with pool.Fori(0, H) as i:
                t.enter(i, 0, PER_SB)
                sb_attention()
                t.leave(H)
            pool.wait_ge(S["rope_in"], 32)
            pool.memset(QM[:, :, :], 0.0)
            pool.drain()
            with pool.Fori(0, H) as i:
                t.enter(i, 0, PER_RET)
                t.take("tab_in", 16)
                pool.wait_ge(S["q_ev"], i + H + 1)
                qp = TAB[:, T_QP:T_QP + P].rearrange("p (o n) -> p o n", o=1).broadcast_to([P, 3, P])
                pool.tensor_tensor(QD[:, :, :], RQT[:, P:SEQ].rearrange("p (c n) -> p c n", c=3), qp, ALU.mult)
                qs = TAB[:, T_QS:T_QS + TS].rearrange("p (o n) -> p o n", o=1).broadcast_to([P, NB, TS])
                diag = QM[:, :, :].rearrange("p b n -> p (b n)")
                diag = bass.AP(diag.tensor, diag.offset, [list(diag.ap[0]), [NS + TS, NB], [1, TS]])
                pool.tensor_tensor(diag, RQT[:, SEQ:T].rearrange("p (b n) -> p b n", b=NB), qs, ALU.mult)\
                    .then_inc(S["qd"], 1)
                t.leave(H)


_INS = ["x_prompt", "x_sample", "state_ret", "cache_sb_k", "cache_sb_v", "page_table", "norm_gain", "w_in",
        "sb_bias", "ret_gn_gain", "w_ret_proj", "w_sb_proj", "w_out", "final_norm_gain"]
_OUTS = [(1, SEQ, D_MODEL), (NB, TS, D_MODEL), (1, 1, H, D, DV), (1, 1, SEQ, H, D), (1, 1, SEQ, H, D),
         (1, NB, H, D, DV), (1, NB, TS, H, D), (1, NB, TS, H, D)]


def constants():
    mats = np.zeros((P, 3, P), np.float32)
    mats[:, 0] = np.eye(P)
    mats[:, 1] = np.tril(np.ones((P, P)))
    mats[:, 2] = 1.0
    half = D // 2
    inv = np.float32(10000.0) ** (-np.arange(half, dtype=np.float32) / np.float32(half))
    pos = np.concatenate([np.arange(SEQ), np.tile(PAGES * P + np.arange(TS), NB)]).astype(np.float32)
    ang = (inv[:, None] * pos[None, :]).astype(np.float32).astype(np.float64)
    rope = np.zeros((2, P, T), np.float32)
    rope[0] = np.concatenate([np.cos(ang), np.cos(ang)])
    rope[1] = np.concatenate([np.sin(ang), -np.sin(ang)])
    tab = np.zeros((H, P, T_W), np.float64)
    i = np.arange(P)
    for h in range(H):
        lg = np.log1p(-np.exp2(-5.0 - h))
        diff = i[None, :] - i[:, None]
        tab[h, :, T_DP:T_DP + P] = np.where(diff >= 0, np.exp(lg * np.maximum(diff, 0)), 0) * SCALE
        s = np.arange(NS)
        ds_ = s[None, :] - s[:, None]
        same = s[None, :] // TS == s[:, None] // TS
        tab[h, 0:NS, T_DS:T_DS + NS] = np.where(same & (ds_ >= 0), np.exp(lg * np.maximum(ds_, 0)), 0) * SCALE
        tab[h, :, T_KP] = np.exp(lg * (P - 1 - i)) * SCALE
        tab[h, 0:NS, T_KS:T_KS + NB] = np.where(s[:, None] // TS == np.arange(NB)[None, :],
                                                np.exp(lg * (TS - 1 - s % TS))[:, None], 0) * SCALE
        tab[h, :, T_GC] = np.exp(lg * P)
        tab[h, :, T_G8] = np.exp(lg * TS)
        tab[h, :, T_QP:T_QP + P] = np.exp(lg * (i + 1))[None, :]
        tab[h, :, T_QS:T_QS + TS] = np.exp(lg * (np.arange(TS) + 1))[None, :]
    return {"const_mats": mats, "const_rope": rope, "const_tab": tab.astype(np.float32)}


def kernel(**inputs):
    import concourse.bacc as bacc
    from concourse.bass_utils import run_bass_kernel_spmd as run

    nc = bacc.Bacc("TRN2", target_bir_lowering=False, num_devices=1, dynamic_dma_scratch_size=1024)
    arrays, args = {}, []
    given = {n: np.ascontiguousarray(inputs[n]) for n in _INS} | constants()
    for name, a in given.items():
        arrays[f"in_{name}"] = a
        args.append(nc.dram_tensor(f"in_{name}", a.shape, mybir.dt.from_np(a.dtype), kind="ExternalInput").ap())
    for n, shape in enumerate(_OUTS):
        args.append(nc.dram_tensor(f"out_{n}", shape, F32, kind="ExternalOutput").ap())
    build(nc, *args)
    r = run(nc, [arrays], core_ids=[0])
    return tuple(r.results[0][f"out_{n}"] for n in range(len(_OUTS)))
```

```python
from contextlib import ExitStack

import numpy as np

import concourse.bass as bass
from concourse import mybir

F32 = mybir.dt.float32
F32R = mybir.dt.float32r
I32 = mybir.dt.int32
ALU = mybir.AluOpType
ACT = mybir.ActivationFunctionType

P = 128
D_MODEL = 2048
SEQ = 512
NB, TS = 8, 8
NS = NB * TS
T = SEQ + NS
HALF = T // 2
H = 8
D = 128
DV = 256
PAGES = 4
KT = D_MODEL // P
QK = 4
C_RQ, C_RK, C_RV, C_RG = 0, 1024, 2048, 4096
C_SQ, C_SK, C_SV, C_SG, C_GR, C_GS = 6144, 7168, 8192, 9216, 10240, 12288
SCALE = float(D) ** -0.5
EPS_RMS, EPS_GN = 1e-6, 1e-5
BIG = 1e38
NO = -1e30
SEG = [(0, 512), (512, 384), (896, 384)]
BLK = [(0, 512), (512, 384), (896, 256), (1152, 128)]
ZS0, ZN0, ZW = 1280, 1536, 1600
T_DP, T_DS, T_KP, T_KS, T_GC, T_G8, T_QP, T_QS, T_KC, T_W = 0, 128, 192, 193, 201, 202, 203, 331, 339, 340

_W = {f"{n}{s}": k for n, k, r in (("raw_in", 16, 2), ("raw_free", 1, 2), ("hi_full", 1, 4), ("w_full", 1, 4),
                                   ("w_free", 1, 4)) for s in range(r)}


def per(loads, act0=0, act1=0, dve0=0, dve1=0, **more):
    out = {k: v * (loads // 2) for k, v in _W.items()}
    return out | {"acc_act0": act0, "acc_act1": act1, "acc_dve0": dve0, "acc_dve1": dve1,
                  "acc_read0": act0 + dve0, "acc_read1": act1 + dve1} | more


PER_SB = per(8, act0=2, act1=2, z_act0=6, z_act1=1, z_act2=1, z_act3=5, z_dve1=5, z_dve2=5, z_dve3=3,
             z_read0=6, z_read1=6, z_read2=6, z_read3=8, q_ev=1, k_ev=1, v_ev=1, qs=1, zq_ready=2, o_ev=1, zs_ready=4,
             w_abs=4, lh_done=3, ll_done=3, w_ln=4, l_raw=4, l_ready=4, x_raw=4, x_ready=4, a_ready=4, t_ready=2, rh_done=2, ge=1, kv_out=64, vn=2,
             **{f"k_in{b}": 64 for b in range(8)}, **{f"v_in{b}": 64 for b in range(8)})
PER_GATE = per(4, act0=1, act1=1, ge=2, sg_ready=2, sg_out0=16, sg_out1=16)
PER_PSB = per(4, dve0=2, dve1=2, gs_in0=32, gs_in1=32, m_ready=4, m_out0=32, m_out1=32)
PER_RET = per(12, act0=2, act1=2, dve0=1, dve1=1, z_act1=1, z_act2=2, z_dve0=3, z_dve1=3, z_dve2=5, z_dve3=4,
              z_read0=3, z_read1=4, z_read2=7, z_read3=4, q_ev=1, k_ev=1, v_ev=2, tab_in=16, tab_used=1, gain_in=16,
              gain_used=1, qd=1, p_ready=2, kd=1, km=1, s_ready=1, st_in0=64, st_in1=64, st_new=4, st_out0=64,
              st_out1=64, vn=4, stat=5, rstd=5, on=5, t_ready=4, rh_done=4, ge=2, rgt_read=2, s_out=16)
PER_C = per(4, dve0=1, dve1=1, mg_in0=32, mg_in1=32, mg_used=2, t_ready=2, rh_done=2, merged=2)
PER_D = per(4, act0=1, act1=1, y_ev=2, z_dve0=1, z_dve1=1, z_dve2=1, z_dve3=1, z_read0=1, z_read1=1, z_read2=1,
            z_read3=1, h_in=64)


class Tally:

    def __init__(self, eng, sems):
        self.eng, self.sems, self.n, self.loop = eng, sems, {}, None

    def value(self, name):
        n = self.n.get(name, 0)
        if self.loop is None:
            return n
        i, first, each, _ = self.loop
        return i * each.get(name, 0) + (n - first * each.get(name, 0))

    def take(self, name, k=1):
        self.n[name] = self.n.get(name, 0) + k
        self.eng.wait_ge(self.sems[name], self.value(name))

    def room(self, name, k=1):
        v = self.value(name)
        if not (isinstance(v, int) and v <= 0):
            self.eng.wait_ge(self.sems[name], v)
        self.n[name] = self.n.get(name, 0) + k

    def reach(self, name):
        self.eng.wait_ge(self.sems[name], self.value(name))

    def settle(self):
        self.eng.sem_inc(self.sems["settled"], 1)

    def skip(self, name, k=1):
        self.n[name] = self.n.get(name, 0) + k

    def enter(self, i, first, each):
        self.loop = (i, first, each, dict(self.n))

    def leave(self, turns):
        _, _, each, before = self.loop
        for name, n in self.n.items():
            one = n - before.get(name, 0)
            assert one == (each.get(name, 0) if one else 0), (name, one, each.get(name, 0))
            self.n[name] = before.get(name, 0) + one * turns
        self.loop = None


def build(nc, x_prompt, x_sample, state_ret, cache_k, cache_v, page_table, norm_gain, w_in, sb_bias, gn_gain,
          w_ret, w_sb, w_out, final_gain, c_mats, c_rope, c_tab,
          y_prompt, y_sample, ret_p, sbk_p, sbv_p, ret_s, sbk_s, sbv_s):
    ctx = ExitStack()
    with ctx:
        names = sorted(set(PER_SB) | set(PER_GATE) | set(PER_PSB) | set(PER_RET) | set(PER_C) | set(PER_D)
                       | {"consts", "mats_r", "vecs", "ng_in", "pt_in", "x_in0", "x_in1", "x_in2", "x_in3", "x_in4",
                          "rs0", "xs_ready", "x_t", "xh_done", "xl_done", "lows_done", "fg_in", "rs_f", "y_done",
                          "y_out", "settled", "rope_in"})
        S = {n: ctx.enter_context(nc.semaphore(n)) for n in names}

        top = [1152]

        def sb(name, shape, dt=F32, at=None):
            size = int(np.prod(shape[1:])) * 4
            if at is None:
                at = top[0]
                top[0] = at + (size + 31) // 32 * 32
            return nc.alloc_sbuf_tensor_at(name, list(shape), dt, offset=at), at + (size + 31) // 32 * 32

        XH, _ = sb("XH", [P, KT, T], F32R)
        XL, _ = sb("XL", [P, KT, T], F32R)
        rh_at = top[0]
        RH, _ = sb("RH", [P, KT, T], F32R)
        RL, _ = sb("RL", [P, KT, T], F32R)
        RAW, _ = sb("RAW", [P, 2, 8, P])
        HI, _ = sb("HI", [P, 4, QK, P], F32R)
        LO, _ = sb("LO", [P, 4, QK, P], F32R)
        MATS, _ = sb("MATS", [P, 3, P])
        NG, _ = sb("NG", [P, KT])
        SBB, _ = sb("SBB", [P, H])
        BIAS, _ = sb("BIAS", [P, 1])
        PT, _ = sb("PT", [1, NB * PAGES], I32)
        SSQ, _ = sb("SSQ", [P, 8])
        RSTD, _ = sb("RSTD", [P, 8])
        IDENT, UPPER, ONES = MATS[:, 0, :], MATS[:, 1, :], MATS[:, 2, :]
        ws = top[0]
        XN, _ = sb("XN", [P, 5, D_MODEL], at=ws)
        JUNK, at = sb("JUNK", [P, D_MODEL], at=rh_at)
        XT, _ = sb("XT", [P, 4, 4, P], at=at)
        KTR, at = sb("KTR", [P, 4, 4 * P], at=rh_at + 8 * T * 4)
        VC, _ = sb("VC", [P, NB, 4 * P], at=rh_at + KT * T * 4 + 8 * T * 4)
        ZQ, at = sb("ZQ", [P, 4 * P], at=at)
        OV, at = sb("OV", [P, 2, P], at=at)
        LH, _ = sb("LH", [P, ZS0], F32R, at=at)
        KC, at = sb("KC", [P, NB, 4 * P], at=ws)
        QT, at = sb("QT", [P, T], at=at)
        KTT, at = sb("KTT", [P, T], at=at)
        VT, at = sb("VT", [P, T], at=at)
        QS, at = sb("QS", [P, NS + 24], at=at)
        KN, at = sb("KN", [P, 5, P], at=at)
        VN, at = sb("VN", [P, 5, P], at=at)
        ZZ, at = sb("ZZ", [P, ZW + 24], at=at)
        LO_, _ = sb("LO_", [P, ZS0], F32R, at=at)
        LL, at = sb("LL", [P, ZW], at=at)
        GG, at = sb("GG", [P, T], at=at)
        GT, at = sb("GT", [P, T], at=at)
        TT, at = sb("TT", [P, T], at=at)
        SG, at = sb("SG", [P, 2, T], at=at)
        MATSR, at = sb("MATSR", [P, 2, P], F32R, at=at)
        assert at <= 229344, at
        RCOS, at = sb("RCOS", [P, T], at=ws)
        RSIN, at = sb("RSIN", [P, T], at=at)
        SG2, _ = sb("SG2", [P, 2, T], at=ws)
        RQT, at = sb("RQT", [P, T], at=at)
        RKT, at = sb("RKT", [P, T], at=at)
        RT, at = sb("RT", [P, T], at=at)
        TAB, at = sb("TAB", [P, T_W], at=at)
        GN2, at = sb("GN2", [P, 2], at=at)
        RVT, at = sb("RVT", [P, T], at=at)
        RVN, at = sb("RVN", [P, 5, DV], at=at)
        KML, _ = sb("KML", [NS, NB, P], F32R, at=at)
        KD, at = sb("KD", [P, 4, P], at=at)
        RGT, at = sb("RGT", [P, T], at=at)
        KM, at = sb("KM", [P, NB, P], F32R, at=at)
        RVS, at = sb("RVS", [P, DV], F32R, at=at)
        RG, at = sb("RG", [P, 2, T], at=at)
        GSI, at2 = sb("GSI", [P, 2, T], at=at)
        MO, at2 = sb("MO", [P, 2, T], at=at2)
        SP_, at = sb("SP_", [P, 4, DV], at=at)
        ST, at = sb("ST", [P, 2, 2, DV], at=at)
        QM, at = sb("QM", [P, NB, NS], at=at)
        QD, at = sb("QD", [P, 3, P], at=at)
        PR, at = sb("PR", [P, 4, P], at=at)
        PS, at = sb("PS", [NS, 2, NS], at=at)
        KS, _ = sb("KS", [NS, P], at=at)
        KSH, _ = sb("KSH", [P, P], F32R, at=at + 4 * P)
        KSL, _ = sb("KSL", [NS, P], F32R, at=at + 8 * P)
        ON, at = sb("ON", [P, 5, DV], at=at)
        STAT, at = sb("STAT", [P, 5, 6], at=at)
        MV, at = sb("MV", [P, 5, 2], at=at)
        RS5, at = sb("RS5", [P, 5], at=at)
        assert at <= 229344, at
        MGI, at = sb("MGI", [P, 2, 2, T], at=ws + 2 * T * 4)
        MT, at = sb("MT", [P, T], at=at)
        HH, _ = sb("HH", [P, 5, D_MODEL], at=rh_at)
        YT, at = sb("YT", [P, 2, T], at=at)
        FG, at = sb("FG", [P, D_MODEL], at=at)
        JF, at = sb("JF", [P, D_MODEL], at=at)
        assert at <= 229344, at

        ACC = [ctx.enter_context(nc.psum_tensor(f"ACC{s}", [P, 2, 512], F32)) for s in range(2)]
        Z = [ctx.enter_context(nc.psum_tensor(f"Z{s}", [P, 512], F32)) for s in range(4)]

        def acc(s):
            return ACC[s][:, :, 0:HALF]

        def one(ap):
            return ap.rearrange("p (o n) -> p o n", o=1)

        def two(ap):
            return ap.rearrange("p (a b) -> p a b", a=2)

        d_gs = nc.dram_tensor("scratch_gate_s", (KT, P, T), F32).ap()
        d_gr = nc.dram_tensor("scratch_gate_r", (KT, P, T), F32).ap()
        d_m = nc.dram_tensor("scratch_merge_s", (KT, P, T), F32).ap()
        block = ctx.enter_context(nc.Block())

        @block.sync
        def _(sp):
            t = Tally(sp, S)
            rot = [0]

            def weights(w, col, half):
                s = rot[0] % 2
                rot[0] += 1
                t.room(f"raw_free{s}")
                src = w[half * 1024:(half + 1) * 1024, bass.ds(col, P)].rearrange("(k p) n -> p k n", p=P)
                sp.dma_start(RAW[:, s], src).then_inc(S[f"raw_in{s}"], 16)

            for n in range(4):
                sp.dma_start(XN[:, n, :], x_prompt[0, n * P:(n + 1) * P, :]).then_inc(S[f"x_in{n}"], 16)
                if n == 0:
                    sp.dma_start(MATS[:], c_mats).then_inc(S["consts"], 16)
                    sp.dma_start(NG[:], norm_gain.rearrange("o (k p) -> p (o k)", p=P),
                                 allow_slow_non_contiguous=True).then_inc(S["ng_in"], 16)
            sp.dma_start(XN[0:NS, 4, :], x_sample.rearrange("b t n -> (b t) n")).then_inc(S["x_in4"], 16)
            weights(w_in[0], C_SQ, 0)
            weights(w_in[0], C_SQ, 1)
            sp.dma_start(SBB[:], sb_bias[0:1, :].broadcast_to([P, H])).then_inc(S["vecs"], 16)
            sp.dma_start(PT[:], page_table.rearrange("b (o n) -> o (b n)", o=1)).then_inc(S["pt_in"], 16)
            sp.wait_ge(S["pt_in"], 16)
            page = [sp.value_load(PT[0:1, k:k + 1], min_val=0, max_val=cache_k.shape[1] - 1)
                    for k in range(NB * PAGES)]

            def keys(h, b):
                for g in range(PAGES):
                    sp.dma_start(KC[:, b, g * P:(g + 1) * P], cache_k[0, page[b * PAGES + g], :, h, :])\
                        .then_inc(S[f"k_in{b}"], 16)

            def values(h, b):
                for g in range(PAGES):
                    sp.dma_start(VC[:, b, g * P:(g + 1) * P], cache_v[0, page[b * PAGES + g], :, h, :])\
                        .then_inc(S[f"v_in{b}"], 16)

            def kv_out(h):
                for g in range(3):
                    t.reach(f"z_read{g}")
                t.settle()
                for src, dp, ds_ in ((KN, sbk_p, sbk_s), (VN, sbv_p, sbv_s)):
                    sp.dma_start(dp[0, 0, :, h, :].rearrange("(n p) d -> p n d", p=P), src[:, 0:4, :])\
                        .then_inc(S["kv_out"], 16)
                    sp.dma_start(ds_[0].rearrange("b t h d -> (b t) h d")[:, h, :], src[0:NS, 4, :])\
                        .then_inc(S["kv_out"], 16)

            K_AT = ((), (), (), (0, 1), (2, 3), (4, 5), (6,), (7,))
            V_AT = ((), (0, 1), (2,), (3,), (), (4,), (5, 6), (7,))

            def cached_values(p, a):
                if p == 1:
                    t.reach("z_read3")
                    t.settle()
                if p == 2:
                    kv_out(a)
                for b in V_AT[p]:
                    values(a, b)

            def cached_keys(p, h, a):
                for b in K_AT[p]:
                    if a is not None:
                        t.take(f"z_read{b % 2}", 1 if b > 1 else 2)
                        t.settle()
                    keys(h, b)

            def sb_body(h, a):
                for p in range(8):
                    if a is not None or p >= 2:
                        weights(w_in[0], (C_SQ, C_SK, C_SV, C_SG)[p // 2] + h * P, p % 2)
                    if a is not None:
                        cached_values(p, a)
                    cached_keys(p, h, a)
                t.skip("z_read0")
                t.skip("z_read1")
                t.skip("z_read2", 1 if a is None else 6)
                t.skip("z_read3", 0 if a is None else 8)

            for g in range(4):
                t.skip(f"z_read{g}", 5)
            sb_body(0, None)
            with sp.Fori(1, H) as i:
                t.enter(i, 1, PER_SB)
                sb_body(i, i - 1)
                t.leave(H - 1)

            gate_n = [0]

            def gate_out(c, dst):
                s = gate_n[0] % 2
                gate_n[0] += 1
                t.take("sg_ready")
                src = (SG if dst is d_gs else SG2)[:, s, :]
                sp.dma_start(dst[c], src).then_inc(S[f"sg_out{s}"], 16)

            for c in range(4):
                for p in range(2):
                    weights(w_in[0], C_GS + c * P, p)
                    cached_values(c * 2 + p, H - 1)
                if c >= 2:
                    gate_out(c - 2, d_gs)
            with sp.Fori(2, 8) as i:
                t.enter(i, 2, PER_GATE)
                for k in range(2):
                    weights(w_in[0], C_GS + (i * 2 + k) * P, 0)
                    weights(w_in[0], C_GS + (i * 2 + k) * P, 1)
                    gate_out(i * 2 + k - 2, d_gs)
                t.leave(6)

            def gate_in(c, s):
                sp.dma_start(GSI[:, s, :], d_gs[c]).then_inc(S[f"gs_in{s}"], 16)

            def merge_part(c, s, more):
                t.take("m_ready")
                sp.dma_start(d_m[c], MO[:, s, :]).then_inc(S[f"m_out{s}"], 16)
                if more:
                    gate_in(c + 2, s)

            sp.wait_ge(S["lows_done"], 1)
            for s in range(2):
                sp.wait_ge(S[f"sg_out{s}"], 16 * 7)
            gate_in(0, 0)
            gate_in(1, 1)
            for k in range(4):
                weights(w_sb[0], k * P, 0)
                if k < 2:
                    gate_out(KT - 2 + k, d_gs)
                if k == 3:
                    merge_part(0, 0, True)
            sp.wait_ge(S["kv_out"], 64 * H)
            sp.dma_start(RCOS[:], c_rope[0]).then_inc(S["rope_in"], 16)
            sp.dma_start(RSIN[:], c_rope[1]).then_inc(S["rope_in"], 16)
            for s in range(2):
                sp.wait_ge(S[f"sg_out{s}"], 16 * 8)
            with sp.Fori(1, 4) as i:
                t.enter(i, 1, PER_PSB)
                for k in range(4):
                    weights(w_sb[0], (i * 4 + k) * P, 0)
                    merge_part(i * 4 + k - 3, (k + 1) % 2, True)
                t.leave(3)

            def tables(h):
                t.room("tab_used")
                sp.dma_start(TAB[:], c_tab[h]).then_inc(S["tab_in"], 16)

            def state_pair(h, j, s):
                t.room(f"st_out{s}", 32)
                for k in range(2):
                    sp.dma_start(ST[:, s, k, :], state_ret[0, 2 * j + k, h, :, :]).then_inc(S[f"st_in{s}"], 16)

            def state_pair_out(h, j, s):
                t.take("st_new")
                for k in range(2):
                    sp.dma_start(ret_s[0, 2 * j + k, h, :, :], ST[:, s, k, :]).then_inc(S[f"st_out{s}"], 16)

            def ret_loads(p, h):
                if p == 6:
                    t.room("gain_used")
                    t.settle()
                    sp.dma_start(GN2[:], gn_gain[0, bass.ds(h * DV, DV)].rearrange("(k p) -> p k", p=P),
                                 allow_slow_non_contiguous=True).then_inc(S["gain_in"], 16)
                if p == 9:
                    tables(h)

            def ret_body(h, a, load):
                for p in range(12):
                    load(p)
                    if p == 0 and a is not None:
                        state_pair(a, 0, 0)
                        state_pair(a, 1, 1)
                    if p == 3 and a is not None:
                        t.take("s_ready")
                        sp.dma_start(ret_p[0, 0, a, :, :], SP_[:, 3, :]).then_inc(S["s_out"], 16)
                    if p in (5, 6) and a is not None:
                        state_pair_out(a, p - 5, (p - 5) % 2)
                        state_pair(a, p - 3, (p - 5) % 2)
                    if p in (7, 8) and a is not None:
                        state_pair_out(a, p - 5, (p - 5) % 2)
                    if h is not None:
                        ret_loads(p, h)

            def ret_cols(h):
                return [C_RQ + h * P, C_RK + h * P, C_RV + h * DV, C_RV + h * DV + P, C_RG + h * DV,
                        C_RG + h * DV + P]

            for p in range(12):
                weights(w_in[0], ret_cols(0)[p // 2], p % 2)
                if p < 3:
                    merge_part(KT - 3 + p, (p + 1) % 2, p == 0)
                if p == 6:
                    for s in range(2):
                        sp.wait_ge(S[f"m_out{s}"], 16 * 8)
                ret_loads(p, 0)
            with sp.Fori(1, H) as i:
                t.enter(i, 1, PER_RET)
                ret_body(i, i - 1, lambda p: weights(w_in[0], ret_cols(i)[p // 2], p % 2))
                t.leave(H - 1)

            def gr_load(p):
                weights(w_in[0], C_GR + (p // 2) * P, p % 2)
                if p % 2 and p >= 5:
                    gate_out(p // 2 - 2, d_gr)

            ret_body(None, H - 1, gr_load)
            with sp.Fori(3, 8) as i:
                t.enter(i, 3, PER_GATE)
                for k in range(2):
                    weights(w_in[0], C_GR + (i * 2 + k) * P, 0)
                    weights(w_in[0], C_GR + (i * 2 + k) * P, 1)
                    gate_out(i * 2 + k - 2, d_gr)
                t.leave(5)

            def merge_in(c, s):
                sp.dma_start(MGI[:, s, 0, :], d_gr[c]).then_inc(S[f"mg_in{s}"], 16)
                sp.dma_start(MGI[:, s, 1, :], d_m[c]).then_inc(S[f"mg_in{s}"], 16)

            sp.wait_ge(S["lows_done"], 2)
            for s in range(2):
                sp.wait_ge(S[f"sg_out{s}"], 16 * 15)
            merge_in(0, 0)
            merge_in(1, 1)
            for k in range(2):
                weights(w_ret[0], 0, k)
                gate_out(KT - 2 + k, d_gr)
            weights(w_ret[0], P, 0)
            weights(w_ret[0], P, 1)
            for s in range(2):
                sp.wait_ge(S[f"sg_out{s}"], 16 * 16)
            with sp.Fori(1, 8) as i:
                t.enter(i, 1, PER_C)
                for k in range(2):
                    weights(w_ret[0], (i * 2 + k) * P, 0)
                    weights(w_ret[0], (i * 2 + k) * P, 1)
                    t.take("mg_used")
                    merge_in(i * 2 + k, k)
                t.leave(7)

            def residual(c):
                cols = bass.ds(c * P, P)
                sp.dma_start(HH[:, 0:4, cols], x_prompt[0, :, cols].rearrange("(n p) d -> p n d", p=P))\
                    .then_inc(S["h_in"], 16)
                sp.dma_start(HH[0:NS, 4, cols], x_sample.rearrange("b t n -> (b t) n")[:, cols])\
                    .then_inc(S["h_in"], 16)

            weights(w_out[0], 0, 0)
            weights(w_out[0], 0, 1)
            sp.wait_ge(S["acc_dve1"], 3 * 8)
            residual(0)
            weights(w_out[0], P, 0)
            residual(1)
            weights(w_out[0], P, 1)
            with sp.Fori(1, 8) as i:
                t.enter(i, 1, PER_D)
                for k in range(2):
                    weights(w_out[0], (i * 2 + k) * P, 0)
                    residual(i * 2 + k)
                    weights(w_out[0], (i * 2 + k) * P, 1)
                t.leave(7)
            for s in range(2):
                sp.wait_ge(S[f"st_out{s}"], 64 * H)
            sp.wait_ge(S["s_out"], 16 * H)
            sp.dma_start(FG[:], final_gain.rearrange("(o n) -> o n", o=1).broadcast_to([P, D_MODEL]))\
                .then_inc(S["fg_in"], 16)
            for n in range(4):
                sp.wait_ge(S["y_done"], n + 1)
                sp.dma_start(y_prompt[0, n * P:(n + 1) * P, :], HH[:, n, :]).then_inc(S["y_out"], 16)
            sp.wait_ge(S["y_done"], 5)
            sp.dma_start(y_sample.rearrange("b t n -> (b t) n"), HH[0:NS, 4, :]).then_inc(S["y_out"], 16)
            sp.wait_ge(S["y_out"], 16 * 5)
            sp.wait_ge(S["kv_out"], 64 * H)
            sp.wait_ge(S["s_out"], 16 * H)
            for s in range(2):
                sp.wait_ge(S[f"st_out{s}"], 64 * H)
                sp.wait_ge(S[f"sg_out{s}"], 16 * 16)
                sp.wait_ge(S[f"m_out{s}"], 16 * 8)

        @block.tensor
        def _(pe):
            t = Tally(pe, S)
            slot, group, unsaid = [0], [0], [None]

            def quarter(xh, xl, k0, first, last, to):
                s, a = slot[0] % 4, group[0] % 2
                slot[0] += 1
                if first:
                    t.room(f"acc_read{a}")
                t.take(f"w_full{s}")
                for k in range(QK):
                    for w, x in ((HI, xh), (HI, xl), (LO, xh)):
                        for half in range(2):
                            mm = pe.matmul(ACC[a][:, half, 0:HALF], w[:, s, k, :],
                                           x[:, k0 + k, half * HALF:(half + 1) * HALF],
                                           start=first and k == 0 and w is HI and x is xh,
                                           stop=last and k == QK - 1 and w is LO)
                            if unsaid[0] is not None:
                                mm.then_inc(S[f"w_free{unsaid[0]}"], 1)
                                unsaid[0] = None
                if last:
                    mm.then_inc(S[f"acc_{to}{a}"], 1)
                    group[0] += 1
                    unsaid[0] = s
                else:
                    mm.then_inc(S[f"w_free{s}"], 1)

            def unit(xh, xl, p, to, units=2):
                for q in range(2):
                    quarter(xh, xl, p * 8 + q * 4, p == 0 and q == 0, p == units - 1 and q == 1, to)

            def transpose(out, in_):
                return pe.transpose(out, in_, IDENT[0:in_.shape[0], 0:in_.shape[0]])

            pe.wait_ge(S["consts"], 16)
            pe.wait_ge(S["mats_r"], 1)
            for n in range(5):
                rows = P if n < 4 else NS
                pe.wait_ge(S["xs_ready"], n + 1)
                for g in range(4):
                    t.room(f"z_read{g}")
                    for k in range(4):
                        mm = transpose(Z[g][:, k * P:k * P + rows], XN[0:rows, n, (4 * g + k) * P:(4 * g + k + 1) * P])
                    mm.then_inc(S[f"z_dve{g}"], 1)

            def cached(b):
                g = b % 2
                t.take(f"k_in{b}", 64)
                t.room(f"z_read{g}")
                for j in range(PAGES):
                    mm = transpose(Z[g][:, j * P:(j + 1) * P], KC[:, b, j * P:(j + 1) * P])
                mm.then_inc(S[f"z_{('act', 'dve')[g]}{g}"], 1)

            def group_logits(g):
                t.reach("z_read0")
                t.reach("z_read1")
                t.room("z_read3")
                for j in range(4):
                    b = 4 * g + j
                    mm = pe.matmul(Z[3][32 * j:32 * j + 32, :], QS[:, b * TS:b * TS + 32], KTR[:, j, :],
                                   start=True, stop=True)
                mm.then_inc(S["z_act3"], 1)

            def group_back():
                t.take("zq_ready")
                t.room("z_read3")
                for c in range(PAGES):
                    mm = transpose(Z[3][:, c * P:(c + 1) * P], ZQ[:, c * P:(c + 1) * P])
                mm.then_inc(S["z_act3"], 1)

            def suffix(j, col, later):
                n = BLK[j][1]
                for jj in (j, *later):
                    oo, m = BLK[jj]
                    for part in (LH, LO_):
                        mm = pe.matmul(Z[2][:, col + n - m:col + n], MATSR[:, 0 if jj == j else 1, :],
                                       part[:, oo:oo + m], start=jj == j and part is LH,
                                       stop=jj == (j, *later)[-1] and part is LO_)
                return mm

            def sb_attention(q):
                if q == 0:
                    t.take("q_ev")
                    t.take("k_ev")
                    for g, blocks in enumerate(((0,), (1,), (2, 3))):
                        t.room(f"z_read{g}")
                        for j in blocks:
                            o, n = BLK[j]
                            c = o - SEG[g][0]
                            mm = pe.matmul(Z[g][:, c:c + n], KTT[:, j * P:(j + 1) * P], QT[:, j * P:SEQ],
                                           start=True, stop=True)
                        mm.then_inc(S[f"z_act{g}"], 1)
                    t.room("z_read3")
                    pe.matmul(Z[3][0:NS, 0:NS], KTT[:, SEQ:T], QT[:, SEQ:T], start=True, stop=True)\
                        .then_inc(S["z_act3"], 1)
                if q in (1, 2, 4, 5):
                    b = {1: 0, 2: 2, 4: 4, 5: 6}[q]
                    cached(b)
                    cached(b + 1)
                if q == 3:
                    t.take("qs")
                    group_logits(0)
                if q == 4:
                    t.skip("l_ready", 3)
                    t.take("lh_done", 3)
                    t.take("ll_done", 3)
                    t.room("z_read2")
                    suffix(0, 0, [1, 2, 3]).then_inc(S["z_dve2"], 1)
                    group_back()
                if q == 5:
                    t.room("z_read2")
                    suffix(1, 0, [2, 3]).then_inc(S["z_dve2"], 1)
                if q == 6:
                    t.room("z_read2")
                    suffix(2, 0, [3])
                    suffix(3, 256, []).then_inc(S["z_dve2"], 1)
                if q == 6:
                    group_logits(1)
                if q == 7:
                    group_back()
                if q == 8:
                    t.take("a_ready", 3)
                    t.take("vn", 2)
                    t.room("z_read2")
                    for j, (o, n) in enumerate(BLK):
                        mm = pe.matmul(Z[2][:, SEQ - n:SEQ], VN[:, j, :], ZZ[:, o:o + n], start=j == 0, stop=j == 3)
                    mm.then_inc(S["z_dve2"], 1)
                if q == 9:
                    t.take("l_ready")
                    t.room("z_read3")
                    ln = LL[0:NS, ZN0:ZW]
                    pe.matmul(Z[3][:, 0:256], UPPER, LL[:, ZS0:ZN0], start=True, stop=False)
                    for c in (3, 2, 1):
                        lc = LL[:, ZS0 + c * NS:ZS0 + (c + 1) * NS].rearrange("p (o n) -> p o n", o=1)
                        pe.matmul(Z[3][:, 0:c * NS].rearrange("p (o n) -> p o n", o=c), ONES,
                                  lc.broadcast_to([P, c, NS]), start=False, stop=False)
                    pe.matmul(Z[3][:, 0:256].rearrange("p (o n) -> p o n", o=4), ONES[0:NS, :],
                              ln.rearrange("p (o n) -> p o n", o=1).broadcast_to([NS, 4, NS]), start=False, stop=True)
                    pe.matmul(Z[3][0:NS, 256:256 + NS], UPPER[0:NS, 0:NS], ln, start=True, stop=True)\
                        .then_inc(S["z_dve3"], 1)
                if q == 11:
                    t.take("a_ready")
                    t.room("z_read3")
                    for g in range(2):
                        for c in range(PAGES + 1):
                            for j in range(4):
                                b = 4 * g + j
                                if c == 0:
                                    t.take(f"v_in{b}", 64)
                                a0 = (ZS0 + c * NS if c < PAGES else ZN0) + b * TS
                                mm = pe.matmul(Z[3][32 * j:32 * j + 32, g * P:(g + 1) * P], ZZ[:, a0:a0 + 32],
                                               VC[:, b, c * P:(c + 1) * P] if c < PAGES else VN[:, 4, :],
                                               start=c == 0, stop=c == PAGES)
                    mm.then_inc(S["z_dve3"], 1)
                if q == 12:
                    t.take("o_ev")
                    t.room("z_read3")
                    for g in range(2):
                        mm = transpose(Z[3][:, g * P:(g + 1) * P], OV[:, g, :])
                    mm.then_inc(S["z_dve3"], 1)

            def sb_new(q):
                if q == 8:
                    pe.wait_ge(S["k_ev"], t.value("k_ev") + 1)
                    t.room("z_read0")
                    for j in range(4):
                        mm = transpose(Z[0][:, j * P:(j + 1) * P], KTT[:, j * P:(j + 1) * P])
                    mm.then_inc(S["z_act0"], 1)
                if q == 12:
                    t.take("v_ev")
                    t.room("z_read2")
                    for j in range(4):
                        mm = transpose(Z[2][:, j * P:(j + 1) * P], VT[:, j * P:(j + 1) * P])
                    mm.then_inc(S["z_dve2"], 1)
                if q == 14:
                    t.room("z_read1")
                    t.settle()
                    transpose(Z[1][0:NS, 0:P], KTT[:, SEQ:T])
                    transpose(Z[1][0:NS, P:2 * P], VT[:, SEQ:T]).then_inc(S["z_dve1"], 1)

            def sb_body(attend, new):
                for q in range(16):
                    if not attend and q < 4:
                        pe.wait_ge(S["xh_done"], 17 + q)
                        pe.wait_ge(S["xl_done"], 17 + q)
                    quarter(XH, XL, q % 4 * 4, q % 4 == 0, q % 4 == 3, "act")
                    if attend:
                        sb_attention(q)
                    if new:
                        sb_new(q)

            sb_body(False, True)
            with pe.Fori(1, H) as i:
                t.enter(i, 1, PER_SB)
                sb_body(True, True)
                t.leave(H - 1)
            sb_body(True, False)
            with pe.Fori(2, 8) as i:
                t.enter(i, 2, PER_GATE)
                for p in range(4):
                    unit(XH, XL, p % 2, "act")
                t.leave(6)

            pe.wait_ge(S["lows_done"], 1)
            with pe.Fori(0, 4) as i:
                t.enter(i, 0, PER_PSB)
                for p in range(4):
                    unit(RH, RL, 0, "dve", units=1)
                t.leave(4)

            def ret_attention(p):
                if p == 0:
                    t.take("q_ev")
                    t.take("k_ev")
                    t.room("z_read0")
                    for c in range(4):
                        mm = pe.matmul(Z[0][:, c * P:(c + 1) * P], RKT[:, c * P:(c + 1) * P],
                                       RQT[:, c * P:(c + 1) * P], start=True, stop=True)
                    mm.then_inc(S["z_dve0"], 1)
                    t.room("z_read3")
                    pe.matmul(Z[3][0:NS, 0:NS], RKT[:, SEQ:T], RQT[:, SEQ:T], start=True, stop=True)
                    transpose(Z[3][0:NS, P:2 * P], RKT[:, SEQ:T]).then_inc(S["z_dve3"], 1)
                    t.room("z_read1")
                    for c in range(4):
                        mm = transpose(Z[1][:, c * P:(c + 1) * P], RKT[:, c * P:(c + 1) * P])
                    mm.then_inc(S["z_act1"], 1)
                if p == 1:
                    t.take("kd")
                    t.take("vn", 4)
                    for g, cc in ((1, (0, 1)), (2, (2, 3))):
                        t.room(f"z_read{g}")
                        for c in cc:
                            mm = pe.matmul(Z[g][:, (c % 2) * DV:(c % 2 + 1) * DV], KD[:, c, :], RVN[:, c, :],
                                           start=True, stop=True)
                        mm.then_inc(S[f"z_dve{g}"], 1)
                if p in (2, 3):
                    g = p - 2
                    if p == 2:
                        t.take("p_ready", 2)
                        t.take("qd")
                        t.take("s_ready")
                    t.room(f"z_read{g}")
                    for c in (2 * g, 2 * g + 1):
                        o = Z[g][:, (c % 2) * DV:(c % 2 + 1) * DV]
                        mm = pe.matmul(o, PR[:, c, :], RVN[:, c, :], start=True, stop=c == 0)
                        if c:
                            mm = pe.matmul(o, QD[:, c - 1, :], SP_[:, c - 1, :], start=False, stop=True)
                    mm.then_inc(S[f"z_dve{g}"], 1)
                if p == 2:
                    t.take("km")
                    t.room("z_read3")
                    t.settle()
                    pe.matmul(Z[3][:, 0:DV], PS[:, :, :].rearrange("p k n -> p (k n)"), RVN[0:NS, 4, :],
                              start=True, stop=False)
                if 2 <= p <= 5:
                    j, s = p - 2, p % 2
                    t.take(f"st_in{s}", 32)
                    for k in range(2):
                        mm = pe.matmul(Z[3][k * NS:(k + 1) * NS, 0:DV], QM[:, 2 * j + k, :], ST[:, s, k, :],
                                       start=False, stop=j == 3)
                    if p == 5:
                        mm.then_inc(S["z_dve3"], 1)
                    t.room("z_read2")
                    for k in range(2):
                        z = Z[2][:, k * DV:(k + 1) * DV]
                        pe.matmul(z, KM[:, 2 * j + k, :], RVS[:, :], start=True, stop=False)
                        mm = pe.matmul(z, KML[:, 2 * j + k, :], RVS[0:NS, :], start=False, stop=True)
                    mm.then_inc(S["z_dve2"], 1)
                if p in (5, 6):
                    g = p - 5
                    if p == 5:
                        t.take("on", 4)
                    t.room(f"z_read{g}")
                    for c in range(4):
                        mm = transpose(Z[g][:, c * P:(c + 1) * P], ON[:, c, g * P:(g + 1) * P])
                    mm.then_inc(S[f"z_dve{g}"], 1)

            def ret_new(p):
                if p in (6, 8):
                    t.take("v_ev")
                    t.room("z_read2")
                    for c in range(4):
                        mm = transpose(Z[2][:, c * P:(c + 1) * P], RVT[:, c * P:(c + 1) * P])
                    mm.then_inc(S["z_act2"], 1)

            def ret_body(attend, new):
                for p in range(12):
                    unit(XH, XL, p % 2, "dve" if new and p < 4 else "act")
                    if attend:
                        ret_attention(p)
                    if new:
                        ret_new(p)
                    if p == 7:
                        t.room("z_read3")
                        if attend:
                            t.take("on")
                            t.settle()
                            for g in range(2):
                                mm = transpose(Z[3][:, g * P:(g + 1) * P], ON[:, 4, g * P:(g + 1) * P])
                        if new:
                            if not attend:
                                t.settle()
                            mm = transpose(Z[3][0:NS, 256:256 + P], RVT[:, SEQ:T])
                        mm.then_inc(S["z_dve3"], 1)
                    if p == 9 and new:
                        t.room("z_read3")
                        t.settle()
                        transpose(Z[3][0:NS, 256:256 + P], RVT[:, SEQ:T]).then_inc(S["z_dve3"], 1)

            ret_body(False, True)
            with pe.Fori(1, H) as i:
                t.enter(i, 1, PER_RET)
                ret_body(True, True)
                t.leave(H - 1)
            ret_body(True, False)
            with pe.Fori(3, 8) as i:
                t.enter(i, 3, PER_GATE)
                for p in range(4):
                    unit(XH, XL, p % 2, "act")
                t.leave(5)

            pe.wait_ge(S["lows_done"], 2)
            with pe.Fori(0, 8) as i:
                t.enter(i, 0, PER_C)
                for p in range(4):
                    unit(RH, RL, p % 2, "dve")
                t.leave(8)

            def back(k):
                t.take("y_ev")
                t.room(f"z_read{k}")
                for n in range(4):
                    mm = transpose(Z[k][:, n * P:(n + 1) * P], YT[:, k, n * P:(n + 1) * P])
                mm.then_inc(S[f"z_dve{k}"], 1)
                t.room(f"z_read{2 + k}")
                t.settle()
                transpose(Z[2 + k][0:NS, 0:P], YT[:, k, SEQ:T]).then_inc(S[f"z_dve{2 + k}"], 1)

            for q in range(8):
                if q in (0, 3):
                    pe.wait_ge(S["merged"], (12, KT)[q // 3])
                quarter(XH, XL, q % 4 * 4, q % 4 == 0, q % 4 == 3, "act")
                if q == 5:
                    back(0)
            with pe.Fori(1, 8) as i:
                t.enter(i, 1, PER_D)
                for p in range(4):
                    unit(XH, XL, p % 2, "act")
                    if p == 0:
                        back(1)
                    if p == 2:
                        back(0)
                t.leave(7)
            back(1)

        @block.scalar
        def _(act):
            t = Tally(act, S)
            splits = [0]

            def split():
                n = splits[0]
                splits[0] += 1
                s, r = n % 4, n // 2 % 2
                if n % 2 == 0:
                    t.take(f"raw_in{r}", 16)
                t.room(f"w_free{s}")
                act.activation(HI[:, s], RAW[:, r, (n % 2) * QK:(n % 2 + 1) * QK, :], ACT.Copy)\
                    .then_inc(S[f"hi_full{s}"], 1)

            act.preload_act_table_set("natural_log_exp_and_others")
            act.wait_ge(S["consts"], 16)
            act.activation(MATSR[:, :, :], MATS[:, 1:3, :], ACT.Copy).then_inc(S["mats_r"], 1)
            for n in range(7):
                if n < 5:
                    rows = P if n < 4 else NS
                    act.wait_ge(S[f"x_in{n}"], 16)
                    act.activation(JUNK[0:rows, :], XN[0:rows, n, :], ACT.Square, accum_out=SSQ[0:rows, n:n + 1])
                    act.drain()
                    act.activation(RSTD[0:rows, n:n + 1], SSQ[0:rows, n:n + 1], ACT.Ln, scale=1.0 / D_MODEL,
                                   bias=EPS_RMS)
                    act.drain()
                    act.activation(RSTD[0:rows, n:n + 1], RSTD[0:rows, n:n + 1], ACT.Exp, scale=-0.5)\
                        .then_inc(S["rs0"], 1)
                if n == 6:
                    for _ in range(3):
                        split()
                if n >= 2:
                    m = n - 2
                    rows = P if m < 4 else NS
                    for g in range(4):
                        act.wait_ge(S["x_t"], 4 * m + g + 1)
                        act.activation(XH[:, 4 * g:4 * g + 4, m * P:m * P + rows], XT[:, g, :, 0:rows], ACT.Copy)\
                            .then_inc(S["xh_done"], 1)
            act.wait_ge(S["vecs"], 16)

            def evacuate(s, dst, ev):
                t.take(f"acc_act{s}")
                act.activation(two(dst[:, :]), acc(s), ACT.Copy).then_inc(S[ev], 1)

            def softplus_tail(lo, hi, parts):
                t.take("w_abs", parts)
                act.activation(LL[:, lo:hi], LL[:, lo:hi], ACT.Exp)
                act.drain()
                act.activation(LL[:, lo:hi], LL[:, lo:hi], ACT.Ln, bias=1.0).then_inc(S["w_ln"], parts)

            def sb_attention(q, a):
                if q == 0:
                    act.activation(BIAS[:, 0:1], SBB[:, bass.ds(a, 1)], ACT.Copy)
                    act.drain()
                    for g, (o, n) in enumerate(SEG):
                        t.take(f"z_act{g}")
                        act.activation(ZZ[:, o:o + n], Z[g][:, 0:n], ACT.Identity, scale=SCALE, bias=BIAS[:, 0:1])\
                            .then_inc(S["zs_ready"], 1)
                        act.drain().then_inc(S[f"z_read{g}"], 1)
                    t.take("z_act3")
                    act.activation(ZZ[0:NS, ZN0:ZW], Z[3][0:NS, 0:NS], ACT.Identity, scale=SCALE,
                                   bias=BIAS[0:NS, 0:1])
                    act.activation(QS[:, 0:NS], QT[:, SEQ:T], ACT.Copy).then_inc(S["qs"], 1)
                    act.drain().then_inc(S["z_read3"], 1)
                if q in (1, 2, 4, 5):
                    b = {1: 0, 2: 2, 4: 4, 5: 6}[q]
                    t.take("z_act0")
                    act.activation(KTR[:, b % 4, :], Z[0][:, :], ACT.Copy)\
                        .then_inc(S["z_read0"], 1)
                if q == 1:
                    softplus_tail(0, ZS0, 3)
                if q == 2:
                    for o, n in SEG:
                        t.take("l_ready")
                        act.activation(LH[:, o:o + n], LL[:, o:o + n], ACT.Copy).then_inc(S["lh_done"], 1)
                    t.skip("l_ready")
                if q in (3, 6):
                    t.take("z_act3")
                    act.activation(ZQ[:, :], Z[3][:, :], ACT.Copy).then_inc(S["zq_ready"], 1)
                    act.drain().then_inc(S["z_read3"], 1)
                if q in (4, 7):
                    g = 0 if q == 4 else 1
                    t.take("z_act3")
                    act.activation(ZZ[:, ZS0:ZN0].rearrange("p (c b t) -> p c b t", c=PAGES, b=NB)
                                   [:, :, 4 * g:4 * g + 4, :],
                                   Z[3][:, :].rearrange("p (c b s) -> p c b s", c=PAGES, b=4)[:, :, :, 0:TS],
                                   ACT.Identity, scale=SCALE, bias=BIAS[:, 0:1])
                    act.drain().then_inc(S["z_read3"], 1)
                if 5 <= q <= 7:
                    o, n = SEG[q - 5]
                    t.take("x_ready")
                    act.activation(ZZ[:, o:o + n], ZZ[:, o:o + n], ACT.Exp).then_inc(S["a_ready"], 1)
                if q == 7:
                    act.drain().then_inc(S["zs_ready"], 1)
                    softplus_tail(ZS0, ZW, 1)
                if q == 9:
                    t.take("t_ready")
                    act.activation(RH[:, bass.ds(a, 1), 0:SEQ], one(TT[:, 0:SEQ]), ACT.Copy)\
                        .then_inc(S["rh_done"], 1)
                if q == 10:
                    t.take("x_ready")
                    act.activation(ZZ[:, ZS0:ZN0], ZZ[:, ZS0:ZN0], ACT.Exp)
                    act.activation(ZZ[0:NS, ZN0:ZW], ZZ[0:NS, ZN0:ZW], ACT.Exp).then_inc(S["a_ready"], 1)
                if q == 12:
                    t.take("t_ready")
                    act.activation(RH[:, bass.ds(a, 1), SEQ:T], one(TT[:, SEQ:T]), ACT.Copy)\
                        .then_inc(S["rh_done"], 1)

            def gate_exp(s, dst):
                t.take(f"acc_act{s}")
                act.activation(two(dst), acc(s), ACT.Exp, scale=-1.0).then_inc(S["ge"], 1)

            def sb_new(q):
                if q == 3:
                    evacuate(0, QT, "q_ev")
                    act.drain().then_inc(S["acc_read0"], 1)
                if q == 7:
                    evacuate(1, KTT, "k_ev")
                    act.drain().then_inc(S["acc_read1"], 1)
                if q == 8:
                    t.room("kv_out", 64)
                    t.take("z_act0")
                    act.activation(KN[:, 0:4, :], Z[0][:, :].rearrange("p (n d) -> p n d", n=4), ACT.Copy)\
                        .then_inc(S["z_read0"], 1)
                if q == 11:
                    evacuate(0, VT, "v_ev")
                    act.drain().then_inc(S["acc_read0"], 1)
                if q == 15:
                    gate_exp(1, GT[:, :])

            def sb_body(a):
                for q in range(16):
                    split()
                    if a is not None:
                        sb_attention(q, a)
                    sb_new(q)

            sb_body(None)
            with act.Fori(1, H) as i:
                t.enter(i, 1, PER_SB)
                sb_body(i - 1)
                t.leave(H - 1)

            gate_n = [0]

            def gate(dst):
                s = gate_n[0] % 2
                gate_n[0] += 1
                t.room(f"sg_out{s}", 16)
                gate_exp(s, dst[:, s, :])
                act.drain().then_inc(S[f"acc_read{s}"], 1)

            for q in range(16):
                split()
                sb_attention(q, H - 1)
                if q % 4 == 3:
                    gate(SG)
            with act.Fori(2, 8) as i:
                t.enter(i, 2, PER_GATE)
                for p in range(4):
                    split()
                    split()
                    if p % 2:
                        gate(SG)
                t.leave(6)
            with act.Fori(0, 4) as i:
                t.enter(i, 0, PER_PSB)
                for p in range(8):
                    split()
                t.leave(4)

            def ret_attention(p, a):
                if p == 0:
                    t.take("tab_in", 16)
                    t.take("z_act1")
                    act.activation(KD[:, :, :], Z[1][:, :].rearrange("p (n d) -> p n d", n=4), ACT.Copy,
                                   scale=TAB[:, T_KP:T_KP + 1]).then_inc(S["kd"], 1)
                    act.drain().then_inc(S["z_read1"], 1)
                if p in (3, 4, 6):
                    for c in {3: (0, 1), 4: (2, 3), 6: (4,)}[p]:
                        t.take("stat")
                        act.activation(RS5[:, c:c + 1], MV[:, c, 1:2], ACT.Ln, bias=EPS_GN)
                        act.drain()
                        act.activation(RS5[:, c:c + 1], RS5[:, c:c + 1], ACT.Exp, scale=-0.5)\
                            .then_inc(S["rstd"], 1)
                if p in (6, 7):
                    g = p - 6
                    t.take("t_ready")
                    act.activation(RH[:, bass.ds(a * 2 + g, 1), 0:SEQ], RT[:, 0:SEQ].rearrange("p (o n) -> p o n", o=1),
                                   ACT.Copy).then_inc(S["rh_done"], 1)
                if p == 8:
                    for g in range(2):
                        t.take("t_ready")
                        act.activation(RH[:, bass.ds(a * 2 + g, 1), SEQ:T],
                                       RT[:, g * NS:(g + 1) * NS].rearrange("p (o n) -> p o n", o=1), ACT.Copy)\
                            .then_inc(S["rh_done"], 1)

            def ret_new(p, attend):
                if p in (5, 7):
                    s = 0 if p == 5 else 1
                    if p == 7:
                        t.take("z_dve3", 3 if attend else 1)
                    evacuate(s, RVT, "v_ev")
                    act.drain().then_inc(S[f"acc_read{s}"], 1)
                if p in (7, 9):
                    g = 0 if p == 7 else 1
                    t.take("z_act2")
                    act.activation(RVN[:, 0:4, g * P:(g + 1) * P], Z[2][:, :].rearrange("p (n d) -> p n d", n=4),
                                   ACT.Copy).then_inc(S["vn"], 1)
                    act.drain().then_inc(S["z_read2"], 1)
                if p == 9:
                    t.skip("z_dve3")
                if p in (9, 11):
                    t.room("rgt_read")
                    gate_exp(0 if p == 9 else 1, RGT[:, :])

            def ret_body(a, new):
                for p in range(12):
                    split()
                    split()
                    if a is not None:
                        ret_attention(p, a)
                    if new:
                        ret_new(p, a is not None)
                    elif p % 2:
                        gate(SG2)

            act.wait_ge(S["rope_in"], 32)
            t.n["z_dve3"] = 5 + 3 * H
            ret_body(None, True)
            with act.Fori(1, H) as i:
                t.enter(i, 1, PER_RET)
                ret_body(i - 1, True)
                t.leave(H - 1)
            ret_body(H - 1, False)
            with act.Fori(3, 8) as i:
                t.enter(i, 3, PER_GATE)
                for p in range(4):
                    split()
                    split()
                    if p % 2:
                        gate(SG2)
                t.leave(5)

            with act.Fori(0, 8) as i:
                t.enter(i, 0, PER_C)
                for p in range(4):
                    split()
                    split()
                    if p % 2:
                        t.take("t_ready")
                        act.activation(XH[:, bass.ds(i * 2 + p // 2, 1), :],
                                       MT[:, :].rearrange("p (o n) -> p o n", o=1), ACT.Copy)\
                            .then_inc(S["rh_done"], 1)
                t.leave(8)

            def out_body(last):
                for p in range(4):
                    for q in range(2):
                        if not (last and 2 * p + q >= 5):
                            split()
                    if p % 2:
                        s = p // 2
                        t.take(f"acc_act{s}")
                        act.activation(two(YT[:, s, :]), acc(s), ACT.Copy).then_inc(S["y_ev"], 1)
                        act.drain().then_inc(S[f"acc_read{s}"], 1)

            with act.Fori(0, 7) as i:
                t.enter(i, 0, PER_D)
                out_body(False)
                t.leave(7)
            out_body(True)
            act.wait_ge(S["fg_in"], 16)
            act.wait_ge(S["lows_done"], 3)
            for n in range(5):
                rows = P if n < 4 else NS
                act.activation(JF[0:rows, :], HH[0:rows, n, :], ACT.Square, accum_out=SSQ[0:rows, n:n + 1])
                act.drain()
                act.activation(RSTD[0:rows, n:n + 1], SSQ[0:rows, n:n + 1], ACT.Ln, scale=1.0 / D_MODEL,
                               bias=EPS_RMS)
                act.drain()
                act.activation(RSTD[0:rows, n:n + 1], RSTD[0:rows, n:n + 1], ACT.Exp, scale=-0.5)\
                    .then_inc(S["rs_f"], 1)

        @block.vector
        def _(dve):
            t = Tally(dve, S)
            splits = [0]

            def split():
                n = splits[0]
                splits[0] += 1
                s, r = n % 4, n // 2 % 2
                t.take(f"hi_full{s}")
                dve.tensor_tensor(LO[:, s], RAW[:, r, (n % 2) * QK:(n % 2 + 1) * QK, :], HI[:, s].bitcast(F32),
                                  ALU.subtract).then_inc(S[f"w_full{s}"], 1)
                if n % 2:
                    dve.drain().then_inc(S[f"raw_free{r}"], 1)

            def scale_rows(n):
                rows = P if n < 4 else NS
                dve.wait_ge(S["rs0"], n + 1)
                dve.tensor_scalar(XN[0:rows, n, :], XN[0:rows, n, :], RSTD[0:rows, n:n + 1], None, ALU.mult)\
                    .then_inc(S["xs_ready"], 1)

            scale_rows(0)
            dve.wait_ge(S["ng_in"], 16)
            for n in range(5):
                rows = P if n < 4 else NS
                if n < 4:
                    scale_rows(n + 1)
                else:
                    for _ in range(3):
                        split()
                for g in range(4):
                    t.take(f"z_dve{g}")
                    if n:
                        dve.wait_ge(S["xl_done"], 4 * (n - 1) + g + 1)
                    dve.tensor_tensor(XT[:, g, :, 0:rows],
                                      Z[g][:, :].rearrange("p (k n) -> p k n", k=4)[:, :, 0:rows],
                                      NG[:, 4 * g:4 * g + 4].rearrange("p (k o) -> p k o", o=1)
                                      .broadcast_to([P, 4, rows]), ALU.mult).then_inc(S["x_t"], 1)
                    dve.drain().then_inc(S[f"z_read{g}"], 1)
            dve.memset(ZZ[:, ZN0:ZW + 24], 0.0)
            dve.memset(QS[:, NS:NS + 24], 0.0)
            dve.memset(VN[:, 4, :], 0.0)

            def negative_abs(lo, hi):
                t.take("zs_ready")
                dve.scalar_tensor_tensor(LL[:, lo:hi], ZZ[:, lo:hi], -1.0, ZZ[:, lo:hi], ALU.mult, ALU.min)\
                    .then_inc(S["w_abs"], 1)

            def log_keep(lo, hi):
                t.take("w_ln")
                dve.scalar_tensor_tensor(LL[:, lo:hi], ZZ[:, lo:hi], 0.0, LL[:, lo:hi], ALU.max, ALU.add)\
                    .then_inc(S["l_raw"], 1)

            def low(dst, src, hi):
                t.take("rh_done")
                dve.tensor_tensor(dst, src, hi.bitcast(F32), ALU.subtract)

            def sb_attention(q, a):
                if q == 0:
                    for o, n in SEG:
                        negative_abs(o, o + n)
                if q in (1, 2, 4, 5):
                    b = {1: 1, 2: 3, 4: 5, 5: 7}[q]
                    t.take("z_dve1")
                    dve.tensor_copy(KTR[:, b % 4, :], Z[1][:, :]).then_inc(S["z_read1"], 1)
                if q == 1:
                    for o, n in SEG:
                        log_keep(o, o + n)
                if 4 <= q <= 6:
                    o, n = SEG[q - 4]
                    t.take("z_dve2")
                    dve.tensor_tensor(ZZ[:, o:o + n], ZZ[:, o:o + n], Z[2][:, 0:n], ALU.subtract)\
                        .then_inc(S["x_raw"], 1)
                    dve.drain().then_inc(S["z_read2"], 1)
                if q == 7:
                    negative_abs(ZS0, ZW)
                if q == 8:
                    log_keep(ZS0, ZW)
                    t.take("z_dve2")
                    dve.tensor_tensor(TT[:, 0:SEQ], Z[2][:, :], GG[:, 0:SEQ], ALU.mult).then_inc(S["t_ready"], 1)
                    dve.drain().then_inc(S["z_read2"], 1)
                if q == 9:
                    low(RL[:, bass.ds(a, 1), 0:SEQ], one(TT[:, 0:SEQ]), RH[:, bass.ds(a, 1), 0:SEQ])
                    t.take("z_dve3")
                    dve.tensor_tensor(ZZ[:, ZS0:ZN0], ZZ[:, ZS0:ZN0], Z[3][:, 0:256], ALU.subtract)
                    dve.tensor_tensor(ZZ[0:NS, ZN0:ZW], ZZ[0:NS, ZN0:ZW], Z[3][0:NS, 256:256 + NS], ALU.subtract)\
                        .then_inc(S["x_raw"], 1)
                    dve.drain().then_inc(S["z_read3"], 1)
                if q == 11:
                    t.take("z_dve3")
                    dve.tensor_copy(OV[:, :, :], Z[3][:, 0:256].rearrange("p (g d) -> p g d", g=2))\
                        .then_inc(S["o_ev"], 1)
                    dve.drain().then_inc(S["z_read3"], 1)
                if q == 12:
                    t.take("z_dve3")
                    by_sample = "p (b t) -> p b t"
                    dve.tensor_tensor(TT[:, SEQ:T].rearrange(by_sample, b=NB),
                                      Z[3][:, 0:256].rearrange("p (b s) -> p b s", b=NB)[:, :, 0:TS],
                                      GG[:, SEQ:T].rearrange(by_sample, b=NB), ALU.mult).then_inc(S["t_ready"], 1)
                    dve.drain().then_inc(S["z_read3"], 1)
                    low(RL[:, bass.ds(a, 1), SEQ:T], one(TT[:, SEQ:T]), RH[:, bass.ds(a, 1), SEQ:T])

            def sigmoid(buf):
                t.take("ge")
                dve.tensor_scalar(buf, buf, BIG, 1.0, ALU.min, ALU.add)
                dve.drain()
                ins = dve.reciprocal(buf, buf)
                return ins

            def sb_new(q):
                if q == 12:
                    t.room("kv_out", 64)
                    t.take("z_dve2")
                    dve.tensor_copy(VN[:, 0:4, :], Z[2][:, :].rearrange("p (n d) -> p n d", n=4))\
                        .then_inc(S["vn"], 1)
                    dve.drain().then_inc(S["z_read2"], 1)
                if q == 14:
                    t.take("z_dve1")
                    dve.tensor_copy(KN[0:NS, 4, :], Z[1][0:NS, 0:P])
                    dve.tensor_copy(VN[0:NS, 4, :], Z[1][0:NS, P:2 * P]).then_inc(S["vn"], 1)
                    dve.drain().then_inc(S["z_read1"], 1)
                if q == 15:
                    sigmoid(GT[:, :])
                    dve.drain()
                    dve.tensor_tensor(two(GG[:, :]), acc(1), two(GT[:, :]), ALU.mult)
                    dve.drain().then_inc(S["acc_read1"], 1)

            def sb_body(a):
                for q in range(16):
                    split()
                    if a is not None:
                        sb_attention(q, a)
                    sb_new(q)

            sb_body(None)
            with dve.Fori(1, H) as i:
                t.enter(i, 1, PER_SB)
                sb_body(i - 1)
                t.leave(H - 1)

            gate_n = [0]

            def gate(dst):
                s = gate_n[0] % 2
                gate_n[0] += 1
                sigmoid(dst[:, s, :]).then_inc(S["sg_ready"], 1)

            for q in range(16):
                split()
                sb_attention(q, H - 1)
                if q % 4 == 3:
                    gate(SG)
            dve.drain().then_inc(S["lows_done"], 1)
            with dve.Fori(2, 8) as i:
                t.enter(i, 2, PER_GATE)
                for p in range(4):
                    split()
                    split()
                    if p % 2:
                        gate(SG)
                t.leave(6)

            with dve.Fori(0, 4) as i:
                t.enter(i, 0, PER_PSB)
                for p in range(4):
                    split()
                    split()
                    s = p % 2
                    t.take(f"gs_in{s}", 16)
                    t.room(f"m_out{s}", 16)
                    t.take(f"acc_dve{s}")
                    dve.tensor_tensor(two(MO[:, s, :]), acc(s), two(GSI[:, s, :]), ALU.mult)
                    dve.drain().then_inc(S[f"acc_read{s}"], 1)
                    dve.drain().then_inc(S["m_ready"], 1)
                t.leave(4)

            def rotary(s, dst, ev):
                t.take(f"acc_dve{s}")
                for lo, hi in ((0, 64), (64, 128)):
                    dve.tensor_tensor(two(RT[hi % 128:hi % 128 + 64, :]), ACC[s][lo:hi, :, 0:HALF],
                                      two(RSIN[lo:hi, :]), ALU.mult)
                dve.tensor_tensor(two(dst[:, :]), acc(s), two(RCOS[:, :]), ALU.mult)
                dve.drain().then_inc(S[f"acc_read{s}"], 1)
                dve.tensor_tensor(dst[:, :], dst[:, :], RT[:, :], ALU.add).then_inc(S[ev], 1)

            def normalise(c, zb, col):
                dve.bn_stats(STAT[:, c, :], zb[:, col:col + DV])
                dve.drain()
                dve.bn_aggr(MV[:, c, :], STAT[:, c, :]).then_inc(S["stat"], 1)

            def apply_norm(c, zb, col):
                t.take("rstd")
                dve.tensor_scalar(ON[:, c, :], zb[:, col:col + DV], MV[:, c, 0:1], RS5[:, c:c + 1],
                                  ALU.subtract, ALU.mult).then_inc(S["on"], 1)

            def by_sample(dst, src, rows):
                return dve.tensor_tensor(dst[:, :, :], one(src[:, :].bitcast(F32)).broadcast_to([rows, NB, P]),
                                         TAB[0:rows, T_KS:T_KS + NB].rearrange("p (b o) -> p b o", o=1)
                                         .broadcast_to([rows, NB, P]), ALU.mult)

            def ret_attention(p, a):
                if p == 0:
                    t.take("tab_in", 16)
                    t.take("z_dve0")
                    dve.tensor_tensor(PR[:, :, :], Z[0][:, :].rearrange("p (c n) -> p c n", c=4),
                                      one(TAB[:, T_DP:T_DP + P]).broadcast_to([P, 4, P]), ALU.mult)\
                        .then_inc(S["p_ready"], 1)
                    dve.drain().then_inc(S["z_read0"], 1)
                    t.take("z_dve3")
                    dve.tensor_tensor(PS[:, :, :], one(Z[3][0:NS, 0:NS]).broadcast_to([NS, 2, NS]),
                                      one(TAB[0:NS, T_DS:T_DS + NS]).broadcast_to([NS, 2, NS]), ALU.mult)\
                        .then_inc(S["p_ready"], 1)
                    dve.tensor_scalar(KS[:, :], Z[3][0:NS, P:2 * P], TAB[0:NS, T_KC:T_KC + 1], None, ALU.mult)
                    dve.drain().then_inc(S["z_read3"], 1)
                    dve.tensor_copy(KSH[0:NS, :], KS[:, :])
                    dve.tensor_copy(KSH[NS:P, :], KS[:, :])
                    dve.tensor_copy(RVS[0:NS, :], RVN[0:NS, 4, :])
                    dve.drain()
                    dve.tensor_tensor(KSL[:, :], KS[:, :], KSH[0:NS, :].bitcast(F32), ALU.subtract)
                    dve.tensor_tensor(RVS[NS:P, :], RVN[0:NS, 4, :], RVS[0:NS, :].bitcast(F32), ALU.subtract)
                    by_sample(KM, KSH, P)
                if p == 1:
                    t.room("s_out", 16)
                    t.take("z_dve1")
                    dve.tensor_copy(SP_[:, 0, :], Z[1][:, 0:DV])
                    dve.drain()
                    dve.scalar_tensor_tensor(SP_[:, 1, :], SP_[:, 0, :], TAB[:, T_GC:T_GC + 1], Z[1][:, DV:2 * DV],
                                             ALU.mult, ALU.add)
                    dve.drain().then_inc(S["z_read1"], 1)
                    t.take("z_dve2")
                    dve.scalar_tensor_tensor(SP_[:, 2, :], SP_[:, 1, :], TAB[:, T_GC:T_GC + 1], Z[2][:, 0:DV],
                                             ALU.mult, ALU.add)
                    dve.drain()
                    dve.scalar_tensor_tensor(SP_[:, 3, :], SP_[:, 2, :], TAB[:, T_GC:T_GC + 1], Z[2][:, DV:2 * DV],
                                             ALU.mult, ALU.add).then_inc(S["s_ready"], 1)
                    dve.drain().then_inc(S["z_read2"], 1)
                    by_sample(KML, KSL, NS).then_inc(S["km"], 1)
                if 2 <= p <= 5:
                    s = p % 2
                    t.take("z_dve2")
                    dve.scalar_tensor_tensor(ST[:, s, :, :], ST[:, s, :, :], TAB[:, T_G8:T_G8 + 1],
                                             Z[2][:, :].rearrange("p (k e) -> p k e", k=2), ALU.mult, ALU.add)\
                        .then_inc(S["st_new"], 1)
                    dve.drain().then_inc(S["z_read2"], 1)
                    if p == 5:
                        dve.drain().then_inc(S["tab_used"], 1)
                if p in (2, 3):
                    g = p - 2
                    t.take(f"z_dve{g}")
                    for c in (2 * g, 2 * g + 1):
                        normalise(c, Z[g], (c % 2) * DV)
                if p in (3, 4):
                    g = p - 3
                    for c in (2 * g, 2 * g + 1):
                        apply_norm(c, Z[g], (c % 2) * DV)
                    dve.drain().then_inc(S[f"z_read{g}"], 1)
                if p == 5:
                    t.take("z_dve3")
                    normalise(4, Z[3], 0)
                if p == 6:
                    apply_norm(4, Z[3], 0)
                    dve.drain().then_inc(S["z_read3"], 1)
                if p in (5, 6):
                    g = p - 5
                    t.take(f"z_dve{g}")
                    dve.tensor_tensor(RT[:, 0:SEQ], Z[g][:, :], RG[:, g, 0:SEQ], ALU.mult).then_inc(S["t_ready"], 1)
                    dve.drain().then_inc(S[f"z_read{g}"], 1)

            def ret_low(g, a):
                low(RL[:, bass.ds(a * 2 + g, 1), 0:SEQ], one(RT[:, 0:SEQ]), RH[:, bass.ds(a * 2 + g, 1), 0:SEQ])
                dve.drain()

            def ret_tail(p, a, new):
                if p == 7:
                    t.take("z_dve3")
                    if new:
                        dve.tensor_copy(RVN[0:NS, 4, 0:P], Z[3][0:NS, 256:256 + P]).then_inc(S["vn"], 1)
                    if a is not None:
                        for g in range(2):
                            by_token = Z[3][:, g * P:(g + 1) * P]
                            by_token = bass.AP(by_token.tensor, by_token.offset,
                                               [list(by_token.ap[0]), [2 * TS, NB // 2], [NS + TS, 2], [1, TS]])
                            pairs = "p (m k t) -> p m k t"
                            dve.tensor_tensor(RT[:, g * NS:(g + 1) * NS].rearrange(pairs, k=2, t=TS), by_token,
                                              RG[:, g, SEQ:T].rearrange(pairs, k=2, t=TS), ALU.mult)\
                                .then_inc(S["t_ready"], 1)
                    dve.drain().then_inc(S["z_read3"], 1)
                if p == 8 and a is not None:
                    for g in range(2):
                        low(RL[:, bass.ds(a * 2 + g, 1), SEQ:T], one(RT[:, g * NS:(g + 1) * NS]),
                            RH[:, bass.ds(a * 2 + g, 1), SEQ:T])
                    dve.drain()
                if p == 9 and new:
                    t.take("z_dve3")
                    dve.tensor_copy(RVN[0:NS, 4, P:2 * P], Z[3][0:NS, 256:256 + P]).then_inc(S["vn"], 1)
                    dve.drain().then_inc(S["z_read3"], 1)

            def ret_new(p, attend):
                if p == 1:
                    if attend:
                        t.take("qd")
                    rotary(0, RQT, "q_ev")
                if p == 3:
                    rotary(1, RKT, "k_ev")
                if p in (9, 11):
                    s = 0 if p == 9 else 1
                    if p == 9:
                        t.take("gain_in", 16)
                    sigmoid(RGT[:, :])
                    dve.drain()
                    dve.scalar_tensor_tensor(two(RG[:, s, :]), acc(s), GN2[:, s:s + 1], two(RGT[:, :]),
                                             ALU.mult, ALU.mult)
                    dve.drain().then_inc(S[f"acc_read{s}"], 1)
                    dve.drain().then_inc(S["rgt_read"], 1)
                    if p == 11:
                        dve.drain().then_inc(S["gain_used"], 1)

            def ret_body(a, new):
                for p in range(12):
                    split()
                    split()
                    if a is not None:
                        if p in (6, 7):
                            ret_low(p - 6, a)
                        ret_attention(p, a)
                    ret_tail(p, a, new)
                    if new:
                        ret_new(p, a is not None)
                    elif p % 2:
                        gate(SG2)

            dve.wait_ge(S["rope_in"], 32)
            ret_body(None, True)
            for s in range(2):
                dve.wait_ge(S[f"m_out{s}"], 16 * 8)
            with dve.Fori(1, H) as i:
                t.enter(i, 1, PER_RET)
                ret_body(i - 1, True)
                t.leave(H - 1)
            ret_body(H - 1, False)
            dve.drain().then_inc(S["lows_done"], 1)
            with dve.Fori(3, 8) as i:
                t.enter(i, 3, PER_GATE)
                for p in range(4):
                    split()
                    split()
                    if p % 2:
                        gate(SG2)
                t.leave(5)

            with dve.Fori(0, 8) as i:
                t.enter(i, 0, PER_C)
                for p in range(4):
                    split()
                    split()
                    if p % 2:
                        s = p // 2
                        c = i * 2 + s
                        t.take(f"mg_in{s}", 32)
                        t.take(f"acc_dve{s}")
                        dve.tensor_tensor(two(MT[:, :]), acc(s), two(MGI[:, s, 0, :]), ALU.mult)
                        dve.drain().then_inc(S[f"acc_read{s}"], 1)
                        dve.tensor_tensor(MT[:, :], MT[:, :], MGI[:, s, 1, :], ALU.add).then_inc(S["t_ready"], 1)
                        dve.drain().then_inc(S["mg_used"], 1)
                        low(XL[:, bass.ds(c, 1), :], one(MT[:, :]), XH[:, bass.ds(c, 1), :])
                        dve.drain().then_inc(S["merged"], 1)
                t.leave(8)

            def add(c, s):
                t.take("h_in", 32)
                t.take(f"z_dve{s}")
                cols = HH[:, 0:4, bass.ds(c * P, P)]
                dve.tensor_tensor(cols, cols, Z[s][:, :].rearrange("p (n d) -> p n d", n=4), ALU.add)
                dve.drain().then_inc(S[f"z_read{s}"], 1)
                t.take(f"z_dve{2 + s}")
                cols = HH[0:NS, 4, bass.ds(c * P, P)]
                dve.tensor_tensor(cols, cols, Z[2 + s][0:NS, 0:P], ALU.add)
                dve.drain().then_inc(S[f"z_read{2 + s}"], 1)

            def out_body(i, first, last):
                for p in range(4):
                    for q in range(2):
                        if not (last and 2 * p + q >= 5):
                            split()
                    if p == 0 and not first:
                        add(i * 2 - 1, 1)
                    if p == 2:
                        add(i * 2, 0)

            out_body(0, True, False)
            with dve.Fori(1, 7) as i:
                t.enter(i, 1, PER_D)
                out_body(i, False, False)
                t.leave(6)
            out_body(7, False, True)
            add(KT - 1, 1)
            dve.drain().then_inc(S["lows_done"], 1)
            dve.wait_ge(S["fg_in"], 16)
            for n in range(5):
                rows = P if n < 4 else NS
                dve.wait_ge(S["rs_f"], n + 1)
                dve.scalar_tensor_tensor(HH[0:rows, n, :], HH[0:rows, n, :], RSTD[0:rows, n:n + 1], FG[0:rows, :],
                                         ALU.mult, ALU.mult).then_inc(S["y_done"], 1)

        @block.gpsimd
        def _(pool):
            t = Tally(pool, S)

            for u in range(20):
                n, g = u // 4, u % 4
                rows = P if n < 4 else NS
                pool.wait_ge(S["xh_done"], u + 1)
                xc = slice(n * P, n * P + rows)
                pool.tensor_tensor(XL[:, 4 * g:4 * g + 4, xc], XT[:, g, :, 0:rows],
                                   XH[:, 4 * g:4 * g + 4, xc].bitcast(F32), ALU.subtract).then_inc(S["xl_done"], 1)

            def causal(buf, o, fill):
                blk = buf[:, o:o + P]
                return pool.affine_select(out=blk, in_=blk, compare_op=ALU.is_gt, fill=fill, base=0,
                                          pattern=[[1, P]], channel_multiplier=-1)

            def causal_new(buf, fill):
                blk = buf[0:NS, ZN0:ZW]
                pool.affine_select(out=blk, in_=blk, compare_op=ALU.is_gt, fill=fill, base=0,
                                   pattern=[[1, NS]], channel_multiplier=-1)
                pool.drain()
                blk = blk.rearrange("p (b t) -> p b t", b=NB)
                return pool.affine_select(out=blk, in_=blk, compare_op=ALU.is_ge, fill=fill, base=0,
                                          pattern=[[-TS, NB], [0, TS]], channel_multiplier=1)

            def mask(buf, fill, raw, ready, g):
                t.take(raw)
                t.settle()
                for o in ((0,), (512,), (896, 1152))[g]:
                    ins = causal(buf, o, fill)
                ins.then_inc(S[ready], 1)

            def sb_attention():
                for g in range(3):
                    mask(LL, 0.0, "l_raw", "l_ready", g)
                for o, n in SEG:
                    t.take("lh_done")
                    pool.tensor_tensor(LO_[:, o:o + n], LL[:, o:o + n], LH[:, o:o + n].bitcast(F32), ALU.subtract)\
                        .then_inc(S["ll_done"], 1)
                for g in range(3):
                    mask(ZZ, NO, "x_raw", "x_ready", g)
                t.take("l_raw")
                t.settle()
                causal_new(LL, 0.0).then_inc(S["l_ready"], 1)
                t.take("x_raw")
                t.settle()
                causal_new(ZZ, NO).then_inc(S["x_ready"], 1)

            with pool.Fori(0, H) as i:
                t.enter(i, 0, PER_SB)
                sb_attention()
                t.leave(H)
            for s in range(2):
                pool.wait_ge(S[f"m_out{s}"], 16 * 8)
            pool.memset(QM[:, :, :], 0.0)
            pool.drain()
            with pool.Fori(0, H) as i:
                t.enter(i, 0, PER_RET)
                t.take("tab_in", 16)
                pool.wait_ge(S["q_ev"], i + H + 1)
                qp = TAB[:, T_QP:T_QP + P].rearrange("p (o n) -> p o n", o=1).broadcast_to([P, 3, P])
                pool.tensor_tensor(QD[:, :, :], RQT[:, P:SEQ].rearrange("p (c n) -> p c n", c=3), qp, ALU.mult)
                qs = TAB[:, T_QS:T_QS + TS].rearrange("p (o n) -> p o n", o=1).broadcast_to([P, NB, TS])
                diag = QM[:, :, :].rearrange("p b n -> p (b n)")
                diag = bass.AP(diag.tensor, diag.offset, [list(diag.ap[0]), [NS + TS, NB], [1, TS]])
                pool.tensor_tensor(diag, RQT[:, SEQ:T].rearrange("p (b n) -> p b n", b=NB), qs, ALU.mult)\
                    .then_inc(S["qd"], 1)
                t.leave(H)


_INS = ["x_prompt", "x_sample", "state_ret", "cache_sb_k", "cache_sb_v", "page_table", "norm_gain", "w_in",
        "sb_bias", "ret_gn_gain", "w_ret_proj", "w_sb_proj", "w_out", "final_norm_gain"]
_OUTS = [(1, SEQ, D_MODEL), (NB, TS, D_MODEL), (1, 1, H, D, DV), (1, 1, SEQ, H, D), (1, 1, SEQ, H, D),
         (1, NB, H, D, DV), (1, NB, TS, H, D), (1, NB, TS, H, D)]


def constants():
    mats = np.zeros((P, 3, P), np.float32)
    mats[:, 0] = np.eye(P)
    mats[:, 1] = np.tril(np.ones((P, P)))
    mats[:, 2] = 1.0
    half = D // 2
    inv = np.float32(10000.0) ** (-np.arange(half, dtype=np.float32) / np.float32(half))
    pos = np.concatenate([np.arange(SEQ), np.tile(PAGES * P + np.arange(TS), NB)]).astype(np.float32)
    ang = (inv[:, None] * pos[None, :]).astype(np.float32).astype(np.float64)
    rope = np.zeros((2, P, T), np.float32)
    rope[0] = np.concatenate([np.cos(ang), np.cos(ang)])
    rope[1] = np.concatenate([np.sin(ang), -np.sin(ang)])
    tab = np.zeros((H, P, T_W), np.float64)
    i = np.arange(P)
    for h in range(H):
        lg = np.log1p(-np.exp2(-5.0 - h))
        diff = i[None, :] - i[:, None]
        tab[h, :, T_DP:T_DP + P] = np.where(diff >= 0, np.exp(lg * np.maximum(diff, 0)), 0) * SCALE
        s = np.arange(NS)
        ds_ = s[None, :] - s[:, None]
        same = s[None, :] // TS == s[:, None] // TS
        tab[h, 0:NS, T_DS:T_DS + NS] = np.where(same & (ds_ >= 0), np.exp(lg * np.maximum(ds_, 0)), 0) * SCALE
        tab[h, :, T_KP] = np.exp(lg * (P - 1 - i)) * SCALE
        own = s // TS
        tab[h, :, T_KS:T_KS + NB] = np.concatenate([own, own])[:, None] == np.arange(NB)[None, :]
        tab[h, 0:NS, T_KC] = np.exp(lg * (TS - 1 - s % TS)) * SCALE
        tab[h, :, T_GC] = np.exp(lg * P)
        tab[h, :, T_G8] = np.exp(lg * TS)
        tab[h, :, T_QP:T_QP + P] = np.exp(lg * (i + 1))[None, :]
        tab[h, :, T_QS:T_QS + TS] = np.exp(lg * (np.arange(TS) + 1))[None, :]
    return {"const_mats": mats, "const_rope": rope, "const_tab": tab.astype(np.float32)}


def kernel(**inputs):
    import concourse.bacc as bacc
    from concourse.bass_utils import run_bass_kernel_spmd as run

    nc = bacc.Bacc("TRN2", target_bir_lowering=False, num_devices=1, dynamic_dma_scratch_size=1024)
    arrays, args = {}, []
    given = {n: np.ascontiguousarray(inputs[n]) for n in _INS} | constants()
    for name, a in given.items():
        arrays[f"in_{name}"] = a
        args.append(nc.dram_tensor(f"in_{name}", a.shape, mybir.dt.from_np(a.dtype), kind="ExternalInput").ap())
    for n, shape in enumerate(_OUTS):
        args.append(nc.dram_tensor(f"out_{n}", shape, F32, kind="ExternalOutput").ap())
    build(nc, *args)
    r = run(nc, [arrays], core_ids=[0])
    return tuple(r.results[0][f"out_{n}"] for n in range(len(_OUTS)))
```
